# Optimizing a Trainium2 kernel written in Bass

```python
import jax, jax.numpy as jnp
from jax import lax
import numpy as np

D_MODEL = 1024
BATCH = 1
SEQ = 256
DEPTH = 2

N_META = 16
BLOCK = 128
PAD = BLOCK - N_META
MLA_HEADS = 8
MLA_NOPE = 64
MLA_ROPE = 32
MLA_QK = MLA_NOPE + MLA_ROPE
MLA_V = 64
Q_LORA = 384
KV_LORA = 256
ROPE_BASE = 10000.0
FOX_HEADS = 8
FOX_DIM = 64
CONV_WIDTH = 3
D_FF = 4 * D_MODEL
EPS = 1e-6
NEG = -1e30
N_EVEN = (DEPTH + 1) // 2
N_ODD = DEPTH // 2
ATTN_SPLITS = (Q_LORA, KV_LORA, MLA_ROPE, FOX_HEADS * FOX_DIM, FOX_HEADS * FOX_DIM, FOX_HEADS * FOX_DIM, FOX_HEADS)
ATTN_IN = Q_LORA + KV_LORA + MLA_ROPE + 3 * FOX_HEADS * FOX_DIM + FOX_HEADS
MIX_OUT = MLA_HEADS * MLA_V + FOX_HEADS * FOX_DIM


def _offsets(sizes):
    out, acc = [], 0
    for s in sizes[:-1]:
        acc += s
        out.append(acc)
    return out

def rms_norm(x, g):
    xf = x.astype(jnp.float32)
    y = xf * lax.rsqrt(jnp.mean(xf * xf, axis=-1, keepdims=True) + EPS)
    return (y * g.astype(jnp.float32)).astype(x.dtype)

def rope_tables(length):
    pos = jnp.arange(length, dtype=jnp.float32)
    inv_freq = ROPE_BASE ** (-jnp.arange(0, MLA_ROPE, 2, dtype=jnp.float32) / MLA_ROPE)
    ang = pos[:, None] * inv_freq[None, :]
    return jnp.cos(ang), jnp.sin(ang)

def rope_tail(x, cos, sin):
    x_nope = x[..., :MLA_NOPE]
    xr = x[..., MLA_NOPE:].astype(jnp.float32)
    x1, x2 = xr[..., : MLA_ROPE // 2], xr[..., MLA_ROPE // 2:]
    c, s = cos[None, :, None, :], sin[None, :, None, :]
    rot = jnp.concatenate([x1 * c - x2 * s, x2 * c + x1 * s], axis=-1).astype(x.dtype)
    return jnp.concatenate([x_nope, rot], axis=-1)

def pad_front(x):
    return jnp.pad(x, [(0, 0), (PAD, 0)] + [(0, 0)] * (x.ndim - 2))

def blocked_causal_attention(q, k, v, scale, cum_log_f=None):
    b, lp, h, dk = q.shape
    nb = lp // BLOCK
    key_pos = jnp.arange(lp)
    qb = q.reshape(b, nb, BLOCK, h, dk).transpose(1, 0, 2, 3, 4)
    use_decay = cum_log_f is not None
    if use_decay:
        f_bh = cum_log_f.transpose(0, 2, 1)
        f_q = f_bh.reshape(b, h, nb, BLOCK).transpose(2, 0, 1, 3)
        xs = (jnp.arange(nb), qb, f_q)
    else:
        xs = (jnp.arange(nb), qb)

    def one_block(args):
        if use_decay:
            i, q_blk, fq = args
        else:
            i, q_blk = args
        s = jnp.einsum('bqhd,bkhd->bhqk', q_blk, k, preferred_element_type=jnp.float32) * scale
        if use_decay:
            s = s + fq[..., :, None] - f_bh[:, :, None, :]
        q_pos = i * BLOCK + jnp.arange(BLOCK)
        mask = (key_pos[None, :] <= q_pos[:, None]) & (key_pos[None, :] >= PAD)
        s = jnp.where(mask[None, None], s, NEG)
        p = jax.nn.softmax(s, axis=-1)
        return jnp.einsum('bhqk,bkhd->bqhd', p.astype(v.dtype), v)

    out = lax.map(one_block, xs)
    return out.transpose(1, 0, 2, 3, 4).reshape(b, lp, h, v.shape[-1])

def attention_mixer(h, cos, sin, w_in, g_cq, w_uq, g_ckv, w_ukv, g_q_mla, g_k_mla,
                    g_q_fox, g_k_fox, b_forget, w_out):
    b, l, _ = h.shape
    z = h @ w_in
    c_q, c_kv, k_pe, fq, fk, fv, f_logit = jnp.split(z, _offsets(ATTN_SPLITS), axis=-1)

    q = (rms_norm(c_q, g_cq) @ w_uq).reshape(b, l, MLA_HEADS, MLA_QK)
    kv = (rms_norm(c_kv, g_ckv) @ w_ukv).reshape(b, l, MLA_HEADS, MLA_NOPE + MLA_V)
    k_nope, v_mla = kv[..., :MLA_NOPE], kv[..., MLA_NOPE:]
    k_rope = jnp.broadcast_to(k_pe[:, :, None, :], (b, l, MLA_HEADS, MLA_ROPE))
    k = jnp.concatenate([k_nope, k_rope], axis=-1)
    q = rope_tail(rms_norm(q, g_q_mla), cos, sin)
    k = rope_tail(rms_norm(k, g_k_mla), cos, sin)
    o_mla = blocked_causal_attention(pad_front(q), pad_front(k), pad_front(v_mla),
                                     MLA_QK ** -0.5)[:, PAD:]
    o_mla = o_mla.reshape(b, l, MLA_HEADS * MLA_V)

    qf = rms_norm(fq.reshape(b, l, FOX_HEADS, FOX_DIM), g_q_fox)
    kf = rms_norm(fk.reshape(b, l, FOX_HEADS, FOX_DIM), g_k_fox)
    vf = fv.reshape(b, l, FOX_HEADS, FOX_DIM)
    log_f = jax.nn.log_sigmoid(f_logit.astype(jnp.float32) + b_forget.astype(jnp.float32))
    cum_log_f = jnp.cumsum(pad_front(log_f), axis=1)
    o_fox = blocked_causal_attention(pad_front(qf), pad_front(kf), pad_front(vf),
                                     FOX_DIM ** -0.5, cum_log_f)[:, PAD:]
    o_fox = o_fox.reshape(b, l, FOX_HEADS * FOX_DIM)

    return jnp.concatenate([o_mla, o_fox], axis=-1) @ w_out

def short_conv_mixer(h, w_in, conv_w, w_out):
    z = h @ w_in
    gate_b, gate_c, u = jnp.split(z, 3, axis=-1)
    g = gate_c * u
    y = lax.conv_general_dilated(
        g, conv_w[:, None, :].astype(g.dtype), window_strides=(1,),
        padding=[(CONV_WIDTH - 1, 0)], dimension_numbers=('NWC', 'WIO', 'NWC'),
        feature_group_count=D_MODEL)
    return (gate_b * y) @ w_out

def sq_relu_mlp(h, w_up, w_down):
    return jnp.square(jax.nn.relu(h @ w_up)) @ w_down

def first_inputs(seed: int = 0) -> dict:
    key = jax.random.key(seed)
    ks = iter(jax.random.split(key, 32))

    def nrm(shape, scale):
        return jax.random.normal(next(ks), shape, jnp.float32) * scale

    def gain(shape):
        return 1.0 + 0.02 * jax.random.normal(next(ks), shape, jnp.float32)

    out_scale = (2.0 * DEPTH) ** -0.5
    return {
        "x": nrm((BATCH, SEQ, D_MODEL), 1.0),
        "meta_tokens": nrm((N_META, D_MODEL), 1.0),
        "g_mix": gain((DEPTH, D_MODEL)),
        "g_mlp": gain((DEPTH, D_MODEL)),
        "w_in_attn": nrm((N_EVEN, D_MODEL, ATTN_IN), D_MODEL ** -0.5),
        "g_cq": gain((N_EVEN, Q_LORA)),
        "w_uq": nrm((N_EVEN, Q_LORA, MLA_HEADS * MLA_QK), Q_LORA ** -0.5),
        "g_ckv": gain((N_EVEN, KV_LORA)),
        "w_ukv": nrm((N_EVEN, KV_LORA, MLA_HEADS * (MLA_NOPE + MLA_V)), KV_LORA ** -0.5),
        "g_q_mla": gain((N_EVEN, MLA_QK)),
        "g_k_mla": gain((N_EVEN, MLA_QK)),
        "g_q_fox": gain((N_EVEN, FOX_DIM)),
        "g_k_fox": gain((N_EVEN, FOX_DIM)),
        "b_forget": 2.0 + nrm((N_EVEN, FOX_HEADS), 0.1),
        "w_out_attn": nrm((N_EVEN, MIX_OUT, D_MODEL), MIX_OUT ** -0.5 * out_scale),
        "w_in_conv": nrm((N_ODD, D_MODEL, 3 * D_MODEL), D_MODEL ** -0.5),
        "conv_w": nrm((N_ODD, CONV_WIDTH, D_MODEL), CONV_WIDTH ** -0.5),
        "w_out_conv": nrm((N_ODD, D_MODEL, D_MODEL), D_MODEL ** -0.5 * out_scale),
        "w_mlp_up": nrm((DEPTH, D_MODEL, D_FF), D_MODEL ** -0.5),
        "w_mlp_down": nrm((DEPTH, D_FF, D_MODEL), D_FF ** -0.5 * out_scale),
    }

def first_block(x, meta_tokens, g_mix, g_mlp, w_in_attn, g_cq, w_uq, g_ckv, w_ukv,
              g_q_mla, g_k_mla, g_q_fox, g_k_fox, b_forget, w_out_attn,
              w_in_conv, conv_w, w_out_conv, w_mlp_up, w_mlp_down):
    b = x.shape[0]
    meta = jnp.broadcast_to(meta_tokens.astype(x.dtype)[None], (b, N_META, D_MODEL))
    h = jnp.concatenate([meta, x], axis=1)
    cos, sin = rope_tables(h.shape[1])
    for layer in range(DEPTH):
        j = layer // 2
        hn = rms_norm(h, g_mix[layer])
        if layer % 2 == 0:
            h = h + attention_mixer(hn, cos, sin, w_in_attn[j], g_cq[j], w_uq[j], g_ckv[j],
                                    w_ukv[j], g_q_mla[j], g_k_mla[j], g_q_fox[j], g_k_fox[j],
                                    b_forget[j], w_out_attn[j])
        else:
            h = h + short_conv_mixer(hn, w_in_conv[j], conv_w[j], w_out_conv[j])
        h = h + sq_relu_mlp(rms_norm(h, g_mlp[layer]), w_mlp_up[layer], w_mlp_down[layer])
    return h[:, N_META:]


N_MIXERS = 2
N_A = (DEPTH + 1) // 2
N_B = DEPTH // 2

CHUNK = 128
A_WIDTH = 2 * D_MODEL
A_GROUPS = 8
A_GDIM = A_WIDTH // A_GROUPS

B_WIDTH = 3 * D_MODEL // 2
B_HEADS = 6
B_HDIM = B_WIDTH // B_HEADS
B_CONV = 4
LRU_C = 8.0

D_FF_2 = 3 * D_MODEL
FFN_CONV = 3


def rms_norm_2(x, g):
    xf = x.astype(jnp.float32)
    y = xf * lax.rsqrt(jnp.mean(xf * xf, axis=-1, keepdims=True) + EPS)
    return (y * g.astype(jnp.float32)).astype(x.dtype)

def causal_dwconv(x, w, b):
    k, c = w.shape
    y = lax.conv_general_dilated(
        x, w.astype(x.dtype)[:, None, :], window_strides=(1,), padding=[(k - 1, 0)],
        dimension_numbers=("NWC", "WIO", "NWC"), feature_group_count=c)
    return y + b.astype(x.dtype)

def mixer_a(h, w_in, v_gain, w_s, b_s, w_out):
    bsz, s, _ = h.shape
    z = jax.nn.gelu(h @ w_in)
    u, v = jnp.split(z, 2, axis=-1)
    v = rms_norm_2(v, v_gain)
    v = v.reshape(bsz, s // CHUNK, CHUNK, A_GROUPS, A_GDIM)
    ws = jnp.tril(w_s).astype(v.dtype)
    sv = jnp.einsum("gts,bcsgd->bctgd", ws, v) + b_s.T.astype(v.dtype)[:, :, None]
    y = u * sv.reshape(bsz, s, A_WIDTH)
    return y @ w_out

def _lin_rec_op(c1, c2):
    a1, b1 = c1
    a2, b2 = c2
    return a1 * a2, a2 * b1 + b2

def mixer_b(h, w_in, conv_w, conv_b, w_a, b_a, w_x, b_x, lam, w_out):
    bsz, s, _ = h.shape
    g, xb = jnp.split(h @ w_in, 2, axis=-1)
    g = jax.nn.gelu(g)
    xb = causal_dwconv(xb, conv_w, conv_b)
    xh = xb.reshape(bsz, s, B_HEADS, B_HDIM)
    r = jax.nn.sigmoid(jnp.einsum("bshd,hde->bshe", xh, w_a) + b_a).reshape(bsz, s, B_WIDTH)
    i = jax.nn.sigmoid(jnp.einsum("bshd,hde->bshe", xh, w_x) + b_x).reshape(bsz, s, B_WIDTH)
    log_a = LRU_C * r.astype(jnp.float32) * jax.nn.log_sigmoid(lam.astype(jnp.float32))
    a = jnp.exp(log_a)
    mult = jnp.sqrt(-jnp.expm1(2.0 * log_a))
    bterm = mult * (i * xb).astype(jnp.float32)
    _, hs = lax.associative_scan(_lin_rec_op, (a, bterm), axis=1)
    y = hs.astype(h.dtype) * g
    return y @ w_out

def conv_ffn(h, w_up, conv_w, conv_b, w_down):
    up = causal_dwconv(h @ w_up, conv_w, conv_b)
    gate, val = jnp.split(up, 2, axis=-1)
    return (jax.nn.gelu(gate) * val) @ w_down

def second_inputs(seed: int = 0) -> dict:
    key = jax.random.key(seed)
    ks = jax.random.split(key, 24)
    nrm = jax.random.normal
    f32 = jnp.float32

    x = nrm(ks[0], (BATCH, SEQ, D_MODEL), f32)
    norm_mix = 1.0 + 0.05 * nrm(ks[1], (DEPTH, D_MODEL), f32)
    norm_ffn = 1.0 + 0.05 * nrm(ks[2], (DEPTH, D_MODEL), f32)
    norm_final = 1.0 + 0.05 * nrm(ks[3], (D_MODEL,), f32)

    a_w_in = nrm(ks[4], (N_A, D_MODEL, 2 * A_WIDTH), f32) * D_MODEL ** -0.5
    a_v_gain = 1.0 + 0.05 * nrm(ks[5], (N_A, A_WIDTH), f32)
    a_w_s = nrm(ks[6], (N_A, A_GROUPS, CHUNK, CHUNK), f32) * (0.5 * CHUNK ** -0.5)
    a_b_s = 1.0 + 0.1 * nrm(ks[7], (N_A, A_GROUPS, CHUNK), f32)
    a_w_out = nrm(ks[8], (N_A, A_WIDTH, D_MODEL), f32) * A_WIDTH ** -0.5

    b_w_in = nrm(ks[9], (N_B, D_MODEL, 2 * B_WIDTH), f32) * D_MODEL ** -0.5
    b_conv_w = nrm(ks[10], (N_B, B_CONV, B_WIDTH), f32) * B_CONV ** -0.5
    b_conv_b = 0.01 * nrm(ks[11], (N_B, B_WIDTH), f32)
    b_w_a = nrm(ks[12], (N_B, B_HEADS, B_HDIM, B_HDIM), f32) * B_HDIM ** -0.5
    b_b_a = 0.01 * nrm(ks[13], (N_B, B_HEADS, B_HDIM), f32)
    b_w_x = nrm(ks[14], (N_B, B_HEADS, B_HDIM, B_HDIM), f32) * B_HDIM ** -0.5
    b_b_x = 0.01 * nrm(ks[15], (N_B, B_HEADS, B_HDIM), f32)
    a0 = jax.random.uniform(ks[16], (N_B, B_WIDTH), f32, 0.9, 0.999)
    s0 = a0 ** (1.0 / LRU_C)
    b_lambda = jnp.log(s0) - jnp.log1p(-s0)
    b_w_out = nrm(ks[17], (N_B, B_WIDTH, D_MODEL), f32) * B_WIDTH ** -0.5

    f_w_up = nrm(ks[18], (DEPTH, D_MODEL, 2 * D_FF_2), f32) * D_MODEL ** -0.5
    f_conv_w = nrm(ks[19], (DEPTH, FFN_CONV, 2 * D_FF_2), f32) * FFN_CONV ** -0.5
    f_conv_b = 0.01 * nrm(ks[20], (DEPTH, 2 * D_FF_2), f32)
    f_w_down = nrm(ks[21], (DEPTH, D_FF_2, D_MODEL), f32) * D_FF_2 ** -0.5

    return {"x": x, "norm_mix": norm_mix, "norm_ffn": norm_ffn, "norm_final": norm_final,
            "a_w_in": a_w_in, "a_v_gain": a_v_gain, "a_w_s": a_w_s, "a_b_s": a_b_s, "a_w_out": a_w_out,
            "b_w_in": b_w_in, "b_conv_w": b_conv_w, "b_conv_b": b_conv_b, "b_w_a": b_w_a, "b_b_a": b_b_a,
            "b_w_x": b_w_x, "b_b_x": b_b_x, "b_lambda": b_lambda, "b_w_out": b_w_out,
            "f_w_up": f_w_up, "f_conv_w": f_conv_w, "f_conv_b": f_conv_b, "f_w_down": f_w_down}

def second_block(x, norm_mix, norm_ffn, norm_final,
              a_w_in, a_v_gain, a_w_s, a_b_s, a_w_out,
              b_w_in, b_conv_w, b_conv_b, b_w_a, b_b_a, b_w_x, b_b_x, b_lambda, b_w_out,
              f_w_up, f_conv_w, f_conv_b, f_w_down):
    for i in range(DEPTH):
        h = rms_norm_2(x, norm_mix[i])
        j = i // N_MIXERS
        if i % N_MIXERS == 0:
            x = x + mixer_a(h, a_w_in[j], a_v_gain[j], a_w_s[j], a_b_s[j], a_w_out[j])
        else:
            x = x + mixer_b(h, b_w_in[j], b_conv_w[j], b_conv_b[j], b_w_a[j], b_b_a[j],
                            b_w_x[j], b_b_x[j], b_lambda[j], b_w_out[j])
        h = rms_norm_2(x, norm_ffn[i])
        x = x + conv_ffn(h, f_w_up[i], f_conv_w[i], f_conv_b[i], f_w_down[i])
    return rms_norm_2(x, norm_final)


def setup_inputs(seed=0):
    out = dict(first_inputs(seed))
    for name, value in second_inputs(seed + 1).items():
        if name != "x":
            out[name + "_2"] = value
    return out


def reference(
    x, meta_tokens, g_mix, g_mlp, w_in_attn, g_cq, w_uq, g_ckv, w_ukv, g_q_mla, g_k_mla,
    g_q_fox, g_k_fox, b_forget, w_out_attn, w_in_conv, conv_w, w_out_conv, w_mlp_up, w_mlp_down,
    norm_mix_2, norm_ffn_2, norm_final_2, a_w_in_2, a_v_gain_2, a_w_s_2, a_b_s_2, a_w_out_2,
    b_w_in_2, b_conv_w_2, b_conv_b_2, b_w_a_2, b_b_a_2, b_w_x_2, b_b_x_2, b_lambda_2, b_w_out_2,
    f_w_up_2, f_conv_w_2, f_conv_b_2, f_w_down_2,
):
    x = first_block(
        x, meta_tokens, g_mix, g_mlp, w_in_attn, g_cq, w_uq, g_ckv, w_ukv, g_q_mla, g_k_mla,
        g_q_fox, g_k_fox, b_forget, w_out_attn, w_in_conv, conv_w, w_out_conv, w_mlp_up,
        w_mlp_down,
    )
    return second_block(
        x, norm_mix_2, norm_ffn_2, norm_final_2, a_w_in_2, a_v_gain_2, a_w_s_2, a_b_s_2,
        a_w_out_2, b_w_in_2, b_conv_w_2, b_conv_b_2, b_w_a_2, b_b_a_2, b_w_x_2, b_b_x_2,
        b_lambda_2, b_w_out_2, f_w_up_2, f_conv_w_2, f_conv_b_2, f_w_down_2,
    )


_drawn_inputs = setup_inputs


def setup_inputs(seed=0):
    import zlib

    import numpy as np

    out = dict(_drawn_inputs(seed))
    spreads = {}
    factors = {'g_mix': 3.1,
     'g_mlp': 2.843,
     'g_cq': 8.0,
     'g_ckv': 8.0,
     'g_q_mla': 8.0,
     'g_k_mla': 8.0,
     'g_q_fox': 8.0,
     'g_k_fox': 8.0,
     'b_forget': 63.408,
     'a_v_gain_2': 55.352,
     'b_conv_b_2': 200.0,
     'b_b_a_2': 200.0,
     'b_b_x_2': 200.0,
     'f_conv_b_2': 55.832,
     'norm_mix_2': 7.354,
     'norm_ffn_2': 8.0,
     'a_b_s_2': 8.0,
     'b_w_a_2': 64.0,
     'b_w_x_2': 47.528,
     'b_lambda_2': 51.944,
     'b_w_in_2': 8.0,
     'b_conv_w_2': 8.0,
     'b_w_out_2': 8.0}
    for name, (base, spread) in spreads.items():
        noise = np.random.default_rng([zlib.crc32(name.encode()), seed]).standard_normal(out[name].shape)
        drawn = base * np.exp(spread * noise) if base else spread * noise
        out[name] = __import__('jax').numpy.asarray(drawn.astype(out[name].dtype))
    for name, factor in factors.items():
        out[name] = (out[name] * factor).astype(out[name].dtype)
    return out
```

```python
from contextlib import ExitStack

import numpy as np

import concourse.bass as bass
from concourse import mybir

F32 = mybir.dt.float32
F32R = mybir.dt.float32r
ACT = mybir.ActivationFunctionType
ALU = mybir.AluOpType
AX = mybir.AxisListType

P = 128
D = 1024
SEQ = 256
META = 16
T0 = SEQ + META
HALO = 2
C1 = META - HALO
T1 = T0 - C1
KT = D // P
HEADS = 8
NOPE, ROPE, QK, DV = 64, 32, 96, 64
FOX_K = 104
EPS = 1e-6
NEG = -1e30
NH1 = 4 * D // P
NH2 = 3 * D // P
NA = 2 * D // P
NB = 3 * D // 2 // P
GROUPS = 8

UB = 8
HLR = 4
RAW = 4
LA = 3

PHASES = [
    ("attn_in", 24, 8, 34), ("attn_out", 8, 8, 8), ("mlp0_up", 32, 8, 32), ("mlp0_down", 32, 8, 8),
    ("conv_in", 24, 8, 24), ("conv_out", 8, 8, 8), ("mlp1_up", 32, 8, 32), ("mlp1_down", 32, 8, 8),
    ("a_v", 16, 8, 16), ("a_u", 16, 8, 16), ("a_out", 16, 8, 8),
    ("f0_up", 48, 8, 48), ("f0_down", 32, 6, 8),
    ("b_in", 32, 8, 48), ("b_out", 16, 6, 8),
    ("f1_up", 48, 8, 48), ("f1_down", 32, 6, 8),
]


class Phase:

    def __init__(self, n, units, blocks, tiles, unit0, tile0):
        self.name, self.units, self.blocks, self.tiles = n, units, blocks, tiles
        self.unit0, self.tile0 = unit0, tile0
        self.bodies = units // UB
        self.next = None


def plan():
    out, u, t = {}, 0, 0
    last = None
    for name, units, blocks, tiles in PHASES:
        ph = Phase(name, units, blocks, tiles, u, t)
        if last:
            last.next = ph
        out[name] = last = ph
        u, t = u + units, t + tiles
    return out


def param_columns():
    sizes = [("g_mix0", 8), ("g_mlp0", 8), ("g_mix1", 8), ("g_mlp1", 8), ("norm_mix0", 8), ("norm_ffn0", 8),
             ("norm_mix1", 8), ("norm_ffn1", 8), ("norm_final", 8), ("g_cq", 3), ("g_ckv", 2), ("g_q_mla", 1),
             ("g_k_mla", 1), ("g_q_fox", 1), ("g_k_fox", 1), ("b_forget", 1), ("eps", 1), ("conv_w", 24),
             ("v_gain", NA), ("b_conv_w", 4 * NB), ("b_conv_b", NB), ("b_b_a", NB), ("b_b_x", NB),
             ("lam", NB), ("f_conv_w0", 3 * 2 * NH2), ("f_conv_b0", 2 * NH2), ("f_conv_w1", 3 * 2 * NH2),
             ("f_conv_b1", 2 * NH2)]
    at, out = 0, {}
    for n, k in sizes:
        out[n] = (at, k)
        at += k
    return out, at


NORM_GAIN = ["g_mix0", "g_mlp0", "g_mix1", "g_mlp1", "norm_mix0", "norm_ffn0", "norm_mix1", "norm_ffn1",
             "norm_final"]
K_IDENT, K_MASK, K_ONES, K_ROPE = 0, P, 2 * P, 3 * P
K_SEL = K_ROPE + T0
NCONST = K_SEL + HEADS
ATANH = [1.0 / 15, 1.0 / 13, 1.0 / 11, 1.0 / 9, 1.0 / 7, 1.0 / 5, 1.0 / 3]


def program(nc, x_in, w8, w6, params_in, consts_in, ws_in, bs_in, out):
    ph = plan()
    pcol, npar = param_columns()
    ctx = ExitStack()
    with ctx:
        def sem(name):
            return ctx.enter_context(nc.semaphore(name))

        def keep(name, shape, dt=F32):
            return ctx.enter_context(nc.sbuf_tensor(name, shape, dt))

        raw = keep("raw", [P, RAW, 2 * UB * P])
        whi = keep("whi", [P, HLR, UB * P], F32R)
        wlo = keep("wlo", [P, HLR, UB * P], F32R)
        h = keep("h", [P, KT, T0])
        xhi = keep("xhi", [P, KT, T0], F32R)
        xlo = keep("xlo", [P, KT, T0], F32R)
        params = keep("params", [P, npar])
        consts = keep("consts", [P, NCONST])
        rstd = keep("rstd", [P, T0])
        root = keep("root", [P, T0])
        ssum = keep("ssum", [P, T0])
        sq = keep("sq", [P, 2, T0])
        xg = keep("xg", [P, 2, T0])
        tmp = keep("tmp", [P, 2, T0])
        log_lam = keep("log_lam", [P, NB])

        with ExitStack() as a:
            def part(name, shape, dt=F32):
                return a.enter_context(nc.sbuf_tensor(name, shape, dt))
            c_raw = part("c_raw", [P, 5, T0])
            chi = part("chi", [P, KT, T0], F32R)
            clo = part("clo", [P, KT, T0], F32R)
            q_mla = part("q_mla", [P, HEADS, T0])
            k_mla = part("k_mla", [P, HEADS, T0])
            q_fox = part("q_fox", [P, HEADS, T0])
            k_fox = part("k_fox", [P, HEADS, T0])
            v_fm = part("v_fm", [P, 2, 4, T0])
            v_tok = part("v_tok", [P, 2, 3, 4 * P])
            wide = part("wide", [P, HEADS * T0])
            inv = part("inv", [P, HEADS, T0])
            rs_c = part("rs_c", [P, 2, T0])
            fg = part("fg", [P, 5, T0])
            soft = part("soft", [P, 2, 4, 3])
        with ExitStack() as a:
            hhi1 = a.enter_context(nc.sbuf_tensor("hhi1", [P, NH1, T1], F32R))
            hlo1 = a.enter_context(nc.sbuf_tensor("hlo1", [P, NH1, T1], F32R))
            act1 = a.enter_context(nc.sbuf_tensor("act1", [P, 2, T1], F32))
            gate_c = a.enter_context(nc.sbuf_tensor("gate_c", [P, KT, T1], F32))
            conv_y = a.enter_context(nc.sbuf_tensor("conv_y", [P, KT, SEQ], F32))
        with ExitStack() as a:
            hhi2 = a.enter_context(nc.sbuf_tensor("hhi2", [P, NH2, SEQ], F32R))
            hlo2 = a.enter_context(nc.sbuf_tensor("hlo2", [P, NH2, SEQ], F32R))
            act2 = a.enter_context(nc.sbuf_tensor("act2", [P, 2, SEQ], F32))
            work1 = a.enter_context(nc.sbuf_tensor("work1", [P, NA, SEQ], F32))
            work2 = a.enter_context(nc.sbuf_tensor("work2", [P, NA * SEQ], F32))
            ws = a.enter_context(nc.sbuf_tensor("ws", [P, GROUPS * P], F32))
            bs = a.enter_context(nc.sbuf_tensor("bs", [P, GROUPS, P], F32))
            work3 = a.enter_context(nc.sbuf_tensor("work3", [P, NB * SEQ], F32))
        v_a, v_atok = work1, work2[:, :].rearrange("p (c n) -> p c n", c=2)
        ws_s = work3[:, 0:2 * GROUPS * P].rearrange("p (c n) -> p c n", c=2)
        xb = work2[:, 0:NB * SEQ].rearrange("p (t n) -> p t n", t=NB)
        decay = work3[:, :].rearrange("p (t n) -> p t n", t=NB)

        def h_gate(t):
            if t < 4:
                return work1[:, NB + t, :]
            if t < 8:
                return work2[:, (NB + t - 4) * SEQ:(NB + t - 3) * SEQ]
            return ws[:, (t - 8) * SEQ:(t - 7) * SEQ]
        cb = work3[:, 0:4 * SEQ].rearrange("p (t n) -> p t n", t=4)
        gg = work3[:, 4 * SEQ:6 * SEQ].rearrange("p (t n) -> p t n", t=2)
        half = work3[:, 6 * SEQ:8 * SEQ].rearrange("p (t n) -> p t n", t=2)

        ps = ctx.enter_context(nc.psum_tensor("ps", [P, 8, 512], F32))

        ident = consts[:, K_IDENT:K_IDENT + P]
        mask = consts[:, K_MASK:K_MASK + P]
        ones = consts[:, K_ONES:K_ONES + P]

        def par(name, i=0, n=1, rows=slice(0, P)):
            a, _ = pcol[name]
            if isinstance(i, int):
                return params[rows, a + i:a + i + n]
            return params[rows, bass.ds(i + a, n)]

        small_in = sem("small_in")
        x_loaded = sem("x_loaded")
        raw_full = [sem(f"raw_full{i}") for i in range(RAW)]
        whi_done = sem("whi_done")
        wlo_done = sem("wlo_done")
        unit_done = sem("unit_done")
        tile_free = sem("tile_free")
        xg_done = sem("xg_done")
        xhi_done = sem("xhi_done")
        xlo_done = sem("xlo_done")
        sq_done = sem("sq_done")
        ssum_done = sem("ssum_done")
        stat_done = sem("stat_done")
        root_done = sem("root_done")
        rstd_done = sem("rstd_done")
        u_done = sem("u_done")
        uhi_done = sem("uhi_done")
        ulo_done = sem("ulo_done")
        out_done = sem("out_done")
        out_ready = sem("out_ready")
        S = {}

        def s(name):
            if name not in S:
                S[name] = sem(name)
            return S[name]

        hid0, at = {}, 0
        for name, n in (("mlp0_up", NH1), ("conv_in", KT), ("mlp1_up", NH1), ("a_u", NA), ("f0_up", NH2),
                        ("b_x", NB), ("b_in", NB), ("f1_up", NH2)):
            hid0[name] = at
            at += n
        made = {"mlp0_down": hid0["mlp0_up"], "conv_out": hid0["conv_in"], "mlp1_down": hid0["mlp1_up"],
                "a_out": hid0["a_u"], "f0_down": hid0["f0_up"], "b_out": hid0["b_in"], "f1_down": hid0["f1_up"]}

        def loop(eng, n, body):
            if n > 1:
                with eng.Fori(0, n) as i:
                    body(i)
            else:
                body(0)

        def loop_ends(eng, n, body):
            body(0, False)
            if n > 3:
                with eng.Fori(1, n - 1) as i:
                    body(i, False)
            elif n == 3:
                body(1, False)
            body(n - 1, True)

        def loop_peeled(eng, n, body):
            if n > 2:
                with eng.Fori(0, n - 1) as i:
                    body(i, False)
            elif n == 2:
                body(0, False)
            body(n - 1, True)

        def split_hi(act, rnd, j, blocks, first=False):
            slot, col, n = (j // 2) % RAW, (j % 2) * blocks * P, blocks * P
            act.wait_ge(raw_full[slot], rnd * 16 + 16)
            if not (first and j < HLR):
                act.wait_ge(unit_done, rnd * UB + (j - HLR + 1))
            nc.scalar.activation(whi[:, j % HLR, 0:n], raw[:, slot, col:col + n], ACT.Copy).then_inc(whi_done, 1)

        def split_lo(dve, rnd, j, blocks):
            slot, col, n = (j // 2) % RAW, (j % 2) * blocks * P, blocks * P
            dve.wait_ge(whi_done, rnd * UB + (j + 1))
            nc.vector.tensor_tensor(wlo[:, j % HLR, 0:n], raw[:, slot, col:col + n],
                                    whi[:, j % HLR, 0:n].bitcast(F32), ALU.subtract).then_inc(wlo_done, 1)

        def ahead(eng, fn, p, it, j, last):
            if p.name in EARLY and isinstance(it, int) and it == j == 0:
                return
            split_ahead(eng, fn, p, it, j, last)

        def split_ahead(eng, fn, p, it, j, last):
            rnd = it + (p.unit0 // UB + (j + LA) // UB)
            blocks = p.blocks
            if last and j + LA >= UB:
                if p.next is None:
                    return
                blocks = p.next.blocks
            fn(eng, rnd, (j + LA) % UB, blocks)

        EARLY = ("attn_in", "mlp0_up", "conv_in", "mlp1_up", "a_v", "b_in")

        def unit(pe, rnd, j, outs, rhs, need=None):
            pe.wait_ge(wlo_done, rnd * UB + (j + 1))
            for b, ((o, start, stop), (xh, xl)) in enumerate(zip(outs, rhs)):
                if need:
                    need(b)
                m = o.shape[0]
                hi = whi[:, j % HLR, b * P:b * P + m]
                lo = wlo[:, j % HLR, b * P:b * P + m]
                nc.tensor.matmul(o, hi, xh, start=start, stop=False)
                nc.tensor.matmul(o, hi, xl, start=False, stop=False)
                mm = nc.tensor.matmul(o, lo, xh, start=False, stop=stop)
            return mm

        def x_rhs(kt, c0, t, hi=xhi, lo=xlo):
            return hi[:, kt, c0:c0 + t], lo[:, kt, c0:c0 + t]

        def pe_wide(pe, p, c0, t, segs, src, made_by, norm=None, after_attention=False):
            per = UB // segs
            ring = 4 if per >= 4 else 2
            ready, base = made_by

            def body(it, first):
                rnd = it + p.unit0 // UB
                for j in range(UB):
                    seg, jt = j % segs, j // segs
                    bank = jt % ring + (4 - ring)
                    if seg == 0 and not (after_attention and jt < 4):
                        pe.wait_ge(tile_free, it * per + (p.tile0 + jt - ring + 1))
                    o = ps[:, bank, 0:t]
                    outs = [(o, seg == 0 and b == 0, seg == segs - 1 and b == p.blocks - 1)
                            for b in range(p.blocks)]
                    rhs = [x_rhs(seg * p.blocks + b, c0, t, *src) for b in range(p.blocks)]
                    need = None
                    if first and jt == 0:
                        def need(b, seg=seg):
                            pe.wait_ge(ready, base + seg * p.blocks + b + 1)
                    unit(pe, rnd, j, outs, rhs, need).then_inc(unit_done, 1)
                    if first and norm is not None and j == 1:
                        pe_stats(pe, norm, c0, t)
            body(0, True)
            if p.bodies > 1:
                with pe.Fori(1, p.bodies) as i:
                    body(i, False)

        def pe_stats(pe, n, c0, t):
            pe.wait_ge(ssum_done, 9 * n + 9)
            nc.tensor.matmul(ps[:, 4, 0:t], ones, ssum[:, c0:c0 + t], start=True, stop=True).then_inc(stat_done, 1)

        def from_x(n):
            return xlo_done, 8 * n

        def from_hidden(name):
            return ulo_done, made[name]

        PRE = (5, 7)

        def act_root(act, n, c0, t, p=None):
            if p:
                split_ahead(act, split_hi, p, 0, 0, False)
            act.wait_ge(stat_done, n + 1)
            nc.scalar.activation(root[:, c0:c0 + t], ps[:, 4, 0:t], ACT.Sqrt, scale=1.0 / D,
                                 bias=par("eps")).then_inc(root_done, 1)

        def dve_rstd(dve, n, c0, t, p=None):
            if p:
                split_ahead(dve, split_lo, p, 0, 0, False)
            dve.wait_ge(root_done, n + 1)
            nc.vector.reciprocal(rstd[:, c0:c0 + t], root[:, c0:c0 + t]).then_inc(rstd_done, 1)
            dve.wait_ge(rstd_done, n + 1)

        def ring2(kt, even):
            return kt % 2 if isinstance(kt, int) else even

        def dve_gain(dve, n, kt, slot, c0, t):
            if not isinstance(kt, int) or 8 * n + kt >= 2:
                dve.wait_ge(xlo_done, kt + (8 * n - 1))
            nc.vector.tensor_scalar(xg[:, slot, 0:t], h[:, kt, c0:c0 + t], par(NORM_GAIN[n], kt), None,
                                    ALU.mult).then_inc(xg_done, 1)

        def act_square(act, n, kt, slot, c0, t):
            if not isinstance(kt, int) or 8 * n + kt >= 2:
                act.wait_ge(ssum_done, kt + (9 * n))
            nc.scalar.activation(sq[:, slot, 0:t], h[:, kt, c0:c0 + t], ACT.Square).then_inc(sq_done, 1)

        def act_xhi(act, n, kt, slot, c0, t):
            act.wait_ge(xg_done, kt + (8 * n + 1))
            nc.scalar.activation(xhi[:, kt, c0:c0 + t], xg[:, slot, 0:t], ACT.Copy).then_inc(xhi_done, 1)

        def pool_clear(pool, n):
            if n:
                pool.wait_ge(stat_done, n)
            nc.gpsimd.memset(ssum[:, :], 0.0).then_inc(ssum_done, 1)

        def pool_xlo(pool, n, kt, slot, c0, t):
            pool.wait_ge(xhi_done, kt + (8 * n + 1))
            nc.gpsimd.tensor_tensor(xlo[:, kt, c0:c0 + t], xg[:, slot, 0:t],
                                    xhi[:, kt, c0:c0 + t].bitcast(F32), ALU.subtract).then_inc(xlo_done, 1)

        def pool_ssum(pool, n, kt, slot, c0, t):
            pool.wait_ge(sq_done, kt + (8 * n + 1))
            pool.wait_ge(ssum_done, kt + (9 * n + 1))
            nc.gpsimd.tensor_tensor(ssum[:, c0:c0 + t], ssum[:, c0:c0 + t], sq[:, slot, 0:t],
                                    ALU.add).then_inc(ssum_done, 1)

        POST = [n for n in range(9) if n not in PRE and n != 8]

        def dve_residual(dve, p, segs, n, c0, t):
            per = UB // segs
            ring = 4 if per >= 4 else 2

            def body(it, last):
                for j in range(UB):
                    if j % segs != segs - 1:
                        ahead(dve, split_lo, p, it, j, last)
                    if j % segs == segs - 1:
                        jt = j // segs
                        kt = it * per + jt
                        dve.wait_ge(unit_done, it * UB + (p.unit0 + j + 1))
                        hh = h[:, kt, c0:c0 + t]
                        nc.vector.tensor_tensor(hh, ps[:, jt % ring + (4 - ring), 0:t], hh,
                                                ALU.add).then_inc(tile_free, 1)
                        if n in POST:
                            dve.wait_ge(tile_free, kt + (p.tile0 + 1))
                            dve_gain(dve, n, kt, jt % 2, c0, t)
                        ahead(dve, split_lo, p, it, j, last)
            loop_peeled(dve, p.bodies, body)

        def act_residual(act, p, segs, n, c0, t):
            per = UB // segs

            def body(it, last):
                for j in range(UB):
                    ahead(act, split_hi, p, it, j, last)
                    if j % segs == segs - 1:
                        jt = j // segs
                        kt = it * per + jt
                        act.wait_ge(tile_free, kt + (p.tile0 + 1))
                        if n in POST:
                            act_xhi(act, n, kt, jt % 2, c0, t)
                        act_square(act, n, kt, jt % 2, c0, t)
            loop_peeled(act, p.bodies, body)

        def pool_residual(pool, p, segs, n, c0, t):
            per = UB // segs
            pool_clear(pool, n)

            def body(it):
                for jt in range(per):
                    kt = it * per + jt
                    if n in POST:
                        pool_xlo(pool, n, kt, jt % 2, c0, t)
                    pool_ssum(pool, n, kt, jt % 2, c0, t)
            loop(pool, p.bodies, body)

        def dve_pre(dve, n, c0, t):
            for kt in range(KT):
                dve.wait_ge(xlo_done, 8 * n + kt - 1)
                nc.vector.scalar_tensor_tensor(out=xg[:, kt % 2, 0:t], in0=h[:, kt, c0:c0 + t],
                                               scalar=par(NORM_GAIN[n], kt), in1=rstd[:, c0:c0 + t],
                                               op0=ALU.mult, op1=ALU.mult).then_inc(xg_done, 1)

        def act_pre(act, n, c0, t):
            for kt in range(KT):
                act_xhi(act, n, kt, kt % 2, c0, t)

        def pool_pre(pool, n, c0, t):
            for kt in range(KT):
                pool_xlo(pool, n, kt, kt % 2, c0, t)

        def dve_mlp_up(dve, p, c0, t):
            def body(it, last):
                for j in range(UB):
                    k = it * UB + j
                    dve.wait_ge(unit_done, k + (p.unit0 + 1))
                    nc.vector.tensor_tensor(tmp[:, j % 2, 0:t], ps[:, j % 4, 0:t], rstd[:, c0:c0 + t],
                                            ALU.mult).then_inc(tile_free, 1)
                    dve.wait_ge(tile_free, k + (p.tile0 + 1))
                    if p.name != "mlp0_up" or not isinstance(it, int):
                        dve.wait_ge(ulo_done, k + (hid0[p.name] - 1))
                    elif k >= 2:
                        dve.wait_ge(ulo_done, k - 1)
                    nc.vector.scalar_tensor_tensor(out=act1[:, j % 2, 0:t], in0=tmp[:, j % 2, 0:t], scalar=0.0,
                                                   in1=tmp[:, j % 2, 0:t], op0=ALU.max,
                                                   op1=ALU.mult).then_inc(u_done, 1)
                    ahead(dve, split_lo, p, it, j, last)
            loop_ends(dve, p.bodies, body)

        def act_hidden(act, p, hi, src, t):
            def body(it, last):
                for j in range(UB):
                    ahead(act, split_hi, p, it, j, last)
                    k = it * UB + j
                    act.wait_ge(u_done, k + (hid0[p.name] + 1))
                    nc.scalar.activation(hi[:, k, 0:t], src[:, j % 2, 0:t], ACT.Copy).then_inc(uhi_done, 1)
            loop_ends(act, p.bodies, body)

        def pool_hidden(pool, p, hi, lo, src, t):
            def body(it):
                for j in range(UB):
                    k = it * UB + j
                    pool.wait_ge(uhi_done, k + (hid0[p.name] + 1))
                    nc.gpsimd.tensor_tensor(lo[:, k, 0:t], src[:, j % 2, 0:t], hi[:, k, 0:t].bitcast(F32),
                                            ALU.subtract).then_inc(ulo_done, 1)
            loop(pool, p.bodies, body)

        def dve_ffn_up(dve, p, layer):
            pairs = UB // 2
            conv, full = s(f"ffn{layer}_first_tap"), s(f"ffn{layer}_second_tap")

            def body(it, last):
                for j in range(UB):
                    k = it * UB + j
                    w = par(f"f_conv_w{layer}", it * (3 * UB) + 3 * j + 1)
                    w0 = par(f"f_conv_w{layer}", it * (3 * UB) + 3 * j)
                    c = cb[:, j % 4, :]
                    dve.wait_ge(conv, k + 1)
                    nc.vector.scalar_tensor_tensor(out=c[:, 1:SEQ], in0=ps[:, j % 4, 0:SEQ - 1], scalar=w,
                                                   in1=c[:, 1:SEQ], op0=ALU.mult, op1=ALU.add).then_inc(full, 1)
                    dve.wait_ge(full, k + 1)
                    nc.vector.scalar_tensor_tensor(out=c[:, 2:SEQ], in0=ps[:, j % 4, 0:SEQ - 2], scalar=w0,
                                                   in1=c[:, 2:SEQ], op0=ALU.mult,
                                                   op1=ALU.add).then_inc(tile_free, 1)
                    ahead(dve, split_lo, p, it, j, last)
            loop_peeled(dve, p.bodies, body)

        def act_ffn_up(act, p, layer):
            pairs = UB // 2
            conv, gated = s(f"ffn{layer}_first_tap"), s(f"ffn{layer}_gelu")

            def body(it, last):
                for j in range(UB):
                    ahead(act, split_hi, p, it, j, last)
                    k = it * UB + j
                    act.wait_ge(unit_done, k + (p.unit0 + 1))
                    if p.name != "f0_up" or not isinstance(it, int) or it * pairs + j // 2 >= 2:
                        act.wait_ge(u_done, it * pairs + (hid0[p.name] + j // 2 - 1))
                    nc.scalar.activation(cb[:, j % 4, :], ps[:, j % 4, 0:SEQ], ACT.Identity,
                                         scale=par(f"f_conv_w{layer}", it * (3 * UB) + 3 * j + 2),
                                         bias=par(f"f_conv_b{layer}", k)).then_inc(conv, 1)
                    if j % 2 == 0:
                        continue
                    pr = it * pairs + j // 2
                    act.wait_ge(tile_free, k + (p.tile0 + 0))
                    nc.scalar.activation(gg[:, (j // 2) % 2, :], cb[:, (j - 1) % 4, :],
                                         ACT.Gelu_apprx_tanh).then_inc(gated, 1)
                    if not isinstance(pr, int) or pr:
                        high(pr - 1, (j // 2 + 1) % 2)

            def high(pr, slot):
                act.wait_ge(u_done, pr + (hid0[p.name] + 1))
                nc.scalar.activation(hhi2[:, pr, :], half[:, slot, :], ACT.Copy).then_inc(uhi_done, 1)
            loop_ends(act, p.bodies, body)
            high(NH2 - 1, (NH2 - 1) % 2)

        def pool_ffn_up(pool, p, layer):
            pairs = UB // 2
            gated = s(f"ffn{layer}_gelu")

            def low(pr, slot):
                pool.wait_ge(uhi_done, pr + (hid0[p.name] + 1))
                nc.gpsimd.tensor_tensor(hlo2[:, pr, :], half[:, slot, :], hhi2[:, pr, :].bitcast(F32),
                                        ALU.subtract).then_inc(ulo_done, 1)

            def body(it, last):
                for i in range(pairs):
                    pr = it * pairs + i
                    pool.wait_ge(gated, pr + 1)
                    pool.wait_ge(ulo_done, pr + (hid0[p.name] - 1))
                    pool.wait_ge(tile_free, it * UB + (p.tile0 + 2 * i + 2))
                    nc.gpsimd.tensor_tensor(half[:, i % 2, :], gg[:, i % 2, :], cb[:, (2 * i + 1) % 4, :],
                                            ALU.mult).then_inc(u_done, 1)
                    if not isinstance(pr, int) or pr:
                        low(pr - 1, (i + 1) % 2)
            loop_ends(pool, p.bodies, body)
            low(NH2 - 1, (NH2 - 1) % 2)

        def dve_log_sigmoid(dve, z, e, t1, t2, res, done, exp_asked, exp_done):
            n = [0]

            def step(ins):
                n[0] += 1
                ins.then_inc(done, 1)
                dve.wait_ge(done, n[0])
            step(nc.vector.scalar_tensor_tensor(out=t1, in0=z, scalar=-1.0, in1=z, op0=ALU.mult, op1=ALU.min))
            nc.vector.tensor_copy(e, t1).then_inc(exp_asked, 1)
            dve.wait_ge(exp_done, 1)
            step(nc.vector.tensor_scalar(t1, e, 2.0, None, ALU.add))
            step(nc.vector.reciprocal(t1, t1))
            step(nc.vector.tensor_tensor(e, e, t1, ALU.mult))
            step(nc.vector.tensor_tensor(t1, e, e, ALU.mult))
            step(nc.vector.tensor_scalar(t2, t1, ATANH[0], None, ALU.mult))
            for c in ATANH[1:]:
                step(nc.vector.scalar_tensor_tensor(out=t2, in0=t2, scalar=c, in1=t1, op0=ALU.add, op1=ALU.mult))
            step(nc.vector.scalar_tensor_tensor(out=t2, in0=t2, scalar=1.0, in1=e, op0=ALU.add, op1=ALU.mult))
            step(nc.vector.tensor_scalar(t1, z, 0.0, None, ALU.min))
            step(nc.vector.scalar_tensor_tensor(out=res, in0=t2, scalar=-2.0, in1=t1, op0=ALU.mult, op1=ALU.add))

        QKS = [
            ("fq", q_fox, NOPE, "g_q_fox"), ("fk", k_fox, NOPE, "g_k_fox"),
            ("k", k_mla, QK, "g_k_mla"), ("q", q_mla, QK, "g_q_mla")]
        U_PE, U_CQ, U_CKV, U_FQ, U_FK, U_FV, U_KN, U_V, U_Q = 0, 1, 4, 6, 10, 14, 18, 19, 20
        TL_CQ, TL_CKV, TL_FQ, TL_FK, TL_FV, TL_KN, TL_V, TL_Q = 1, 4, 6, 10, 14, 18, 22, 26
        N_TL = 34
        tile_unit = (list(range(18)) + [U_KN] * 4 + [U_V] * 4 + [U_Q + (3 * hd + 2) // 8 for hd in range(HEADS)])
        prob = [wide[:, i * 656:(i + 1) * 656] for i in range(2)]
        prob_t = [wide[:, 1312 + i * 432:1312 + (i + 1) * 432] for i in range(2)]
        wide3 = wide[:, :].rearrange("p (h n) -> p h n", h=HEADS)
        c_ss, c_root, c_rstd = s("latent_stat"), s("latent_root"), s("latent_rstd")
        c_sq, c_g, c_hi, c_lo = s("latent_square"), s("latent_gain"), s("latent_hi"), s("latent_lo")
        n_sq, n_ss, n_root, n_inv, n_out = (s("head_square"), s("head_stat"), s("head_root"), s("head_inverse"),
                                            s("head_normed"))
        rope_done, kpe_done = s("rope_done"), s("kpe_copied")
        vt_ps, vt_done = s("v_turned"), s("v_tok_done")
        fox_done, fox_pad = s("fox_rows_done"), s("fox_rows_cleared")
        sc_done, mx_done, nb_done, ex_done = s("scores_done"), s("max_done"), s("minus_max"), s("exp_done")
        rc_done, pn_done, pt_ps, pt_done = s("sum_inverse"), s("prob_done"), s("prob_turned"), s("prob_t_done")
        pv_done, ohi_done, olo_done = s("pv_done"), s("ohi_done"), s("olo_done")
        HALF = [slice(0, 64), slice(64, 128)]
        heads = [("k", q_mla, k_mla, QK, QK ** -0.5, 0, i) for i in range(HEADS)] + \
                [("f", q_fox, k_fox, FOX_K, NOPE ** -0.5, 1, i) for i in range(HEADS)]
        NHD = len(heads)
        SPAN = [(0, P, 0), (P, 2 * P, P), (2 * P, T0, 3 * P)]

        block = ctx.enter_context(nc.Block())

        @block.sync
        def _(sp):
            sp.dma_start(params[:, :], params_in).then_inc(small_in, 16)
            sp.dma_start(h[:, :, :], x_in).then_inc(x_loaded, 16)
            sp.dma_start(consts[:, :], consts_in).then_inc(small_in, 16)

            def slabs(src, first, n, cols, rnd0):
                def body(i, wait=True):
                    for k in range(RAW):
                        if wait:
                            sp.wait_ge(wlo_done, i * UB + ((rnd0 - 1) * UB + 2 * k + 2))
                        sp.dma_start(raw[:, k, 0:cols], src[first + k + i * RAW]).then_inc(raw_full[k], 16)
                if rnd0 == 0:
                    body(0, wait=False)
                    with sp.Fori(1, n) as i:
                        body(i)
                else:
                    with sp.Fori(0, n) as i:
                        body(i)
            at = {8: 0, 6: 0}
            names = list(ph)
            g = 0
            while g < len(names):
                e = g
                while e < len(names) and ph[names[e]].blocks == ph[names[g]].blocks:
                    e += 1
                blocks = ph[names[g]].blocks
                n = sum(ph[x].bodies for x in names[g:e])
                slabs(w8 if blocks == 8 else w6, at[blocks], n, 2 * blocks * P, ph[names[g]].unit0 // UB)
                at[blocks] += n * RAW
                g = e
            for kt in range(KT):
                sp.wait_ge(out_ready, kt + 1)
                sp.dma_start(out[:, kt, :], h[:, kt, META:T0]).then_inc(out_done, 16)
            sp.wait_ge(out_done, 16 * KT)

        @block.tensor
        def _(pe):
            p = ph["attn_in"]
            pe.wait_ge(small_in, 32)
            t = [0]

            def take():
                if t[0] >= 4:
                    pe.wait_ge(tile_free, t[0] - 3)
                t[0] += 1
                return (t[0] - 1) % 4

            def whole(u):
                bank = take()
                need = (lambda b: pe.wait_ge(xlo_done, b + 1)) if u == 0 else None
                mm = unit(pe, u // UB, u % UB, [(ps[:, bank, 0:T0], b == 0, b == 7) for b in range(8)],
                          [x_rhs(b, 0, T0) for b in range(8)], need)
                mm.then_inc(unit_done, 1)
                if u == 1:
                    pe_stats(pe, 0, 0, T0)

            for u in range(0, U_FQ + 1):
                whole(u)
            pe.wait_ge(c_sq, 5)
            for i in range(5):
                mm = nc.tensor.matmul(ps[:, 4 + (i >= 3), 0:T0], ones, wide3[:, i, :], start=i in (0, 3),
                                      stop=i in (2, 4))
                if i in (2, 4):
                    mm.then_inc(c_ss, 1)

            def head_stats(n, rows):
                pe.wait_ge(n_sq, n + 1)
                for hd in range(HEADS):
                    k = n * HEADS + hd
                    if k >= 2:
                        pe.wait_ge(n_root, k - 1)
                    nc.tensor.matmul(ps[:, 6 + k % 2, 0:T0], ones[0:rows, :], wide3[0:rows, hd, :], start=True,
                                     stop=True).then_inc(n_ss, 1)

            for u in range(U_FQ + 1, U_FV):
                whole(u)
            head_stats(0, NOPE)
            for u in range(U_FV, U_KN):
                whole(u)
            head_stats(1, NOPE)

            pe.wait_ge(c_lo, 5)
            for u in (U_KN, U_V):
                pe.wait_ge(wlo_done, u + 1)
                for i in range(4):
                    bank = take()
                    o = ps[:, bank, 0:T0]
                    for kt in range(2):
                        b = 2 * i + kt
                        xh, xl = x_rhs(3 + kt, 0, T0, chi, clo)
                        hi, lo = whi[:, u % HLR, b * P:b * P + P], wlo[:, u % HLR, b * P:b * P + P]
                        nc.tensor.matmul(o, hi, xh, start=kt == 0, stop=False)
                        nc.tensor.matmul(o, hi, xl, start=False, stop=False)
                        mm = nc.tensor.matmul(o, lo, xh, start=False, stop=kt == 1)
                    if i == 3:
                        mm.then_inc(unit_done, 1)
                    else:
                        mm.then_inc(s("inner_tile"), 1)
            for hd in range(HEADS):
                bank = take()
                o = ps[:, bank, 0:T0]
                for kt in range(3):
                    g = 3 * hd + kt
                    u, b = U_Q + g // 8, g % 8
                    if b == 0:
                        pe.wait_ge(wlo_done, u + 1)
                    if g == 3 * HEADS - 1:
                        pe.wait_ge(wlo_done, u + 2)
                    xh, xl = x_rhs(kt, 0, T0, chi, clo)
                    hi, lo = whi[:, u % HLR, b * P:b * P + P], wlo[:, u % HLR, b * P:b * P + P]
                    nc.tensor.matmul(o, hi, xh, start=kt == 0, stop=False)
                    nc.tensor.matmul(o, hi, xl, start=False, stop=False)
                    mm = nc.tensor.matmul(o, lo, xh, start=False, stop=kt == 2)
                    if b == 7:
                        mm.then_inc(unit_done, 2 if u == U_Q + 2 else 1)
                    elif kt == 2:
                        mm.then_inc(s("inner_tile"), 1)
            head_stats(2, QK)
            for w in range(2):
                pe.wait_ge(tile_free, (TL_FV + 4) if w else (TL_V + 4))
                for kt, (a, n) in enumerate(((0, P), (P, P), (2 * P, META))):
                    k = 3 * w + kt
                    if k >= 2:
                        pe.wait_ge(vt_done, k - 1)
                    for i in range(4):
                        mm = nc.tensor.transpose(ps[0:n, 4 + k % 2, i * P:(i + 1) * P], v_fm[:, w, i, a:a + n],
                                                 ident)
                    mm.then_inc(vt_ps, 1)
            head_stats(3, QK)

            def scores(i):
                kind, q, k, rows, _, _, hd = heads[i]
                b = 4 * (i % 2)
                if i == 0:
                    pe.wait_ge(rope_done, 6)
                    pe.wait_ge(tile_free, N_TL)
                    pe.wait_ge(n_root, 4 * HEADS)
                    pe.wait_ge(vt_done, 6)
                    pe.wait_ge(n_out, 4)
                if kind == "f" and hd == 0:
                    pe.wait_ge(fox_done, 4)
                if i >= 2:
                    pe.wait_ge(ex_done, 3 * (i - 1))
                for r, (a, to, _) in enumerate(SPAN):
                    n = min(P, T0 - a)
                    o = ps[0:n, b, a:a + to] if r < 2 else ps[0:n, b + 1, 0:to]
                    nc.tensor.matmul(o, q[0:rows, hd, a:a + n], k[0:rows, hd, 0:to], start=True, stop=False)
                    mm = nc.tensor.matmul(o[:, a:to], ident[:, 0:n], mask[:, 0:n], start=False, stop=True)
                mm.then_inc(sc_done, 1)

            def turn(i):
                b = 4 * (i % 2) + 2
                pr = prob[i % 2]
                pe.wait_ge(pn_done, 3 * i + 3)
                if i >= 2:
                    pe.wait_ge(pt_done, 2 * (i - 1))
                at = 0
                for kt in range(3):
                    nk = min(P, T0 - kt * P)
                    for r in range(kt, 3):
                        a, to, col = SPAN[r]
                        n = min(P, T0 - a)
                        mm = nc.tensor.transpose(ps[0:nk, b, at:at + n], pr[0:n, col + kt * P:col + kt * P + nk],
                                                 ident[0:n, 0:n])
                        at += n
                mm.then_inc(pt_ps, 1)

            def values(i):
                _, _, _, _, _, w, hd = heads[i]
                b = 4 * (i % 2) + 3
                pt = prob_t[i % 2]
                pe.wait_ge(pt_done, 2 * i + 2)
                if i >= 2:
                    pe.wait_ge(olo_done, i - 1)
                r0 = 64 * (hd % 2)
                at = 0
                for kt in range(3):
                    nk = min(P, T0 - kt * P)
                    n = T0 - kt * P
                    mm = nc.tensor.matmul(ps[r0:r0 + DV, b, kt * P:T0], v_tok[0:nk, w, kt, hd * DV:(hd + 1) * DV],
                                          pt[0:nk, at:at + n], start=kt == 0, stop=kt == 2)
                    at += n
                mm.then_inc(pv_done, 1)

            for st in range(NHD + 2):
                if st < NHD:
                    scores(st)
                if 1 <= st <= NHD:
                    turn(st - 1)
                if st >= 2:
                    values(st - 2)

            pe_wide(pe, ph["attn_out"], C1, T1, 1, (chi, clo), (olo_done, NHD - UB), after_attention=True)
            pe_wide(pe, ph["mlp0_up"], C1, T1, 1, (xhi, xlo), from_x(1), norm=1)
            pe_wide(pe, ph["mlp0_down"], 0, T1, 4, (hhi1, hlo1), from_hidden("mlp0_down"))
            pe_wide(pe, ph["conv_in"], C1, T1, 1, (xhi, xlo), from_x(2), norm=2)
            pe_wide(pe, ph["conv_out"], 0, SEQ, 1, (hhi1, hlo1), from_hidden("conv_out"))
            pe_wide(pe, ph["mlp1_up"], META, SEQ, 1, (xhi, xlo), from_x(3), norm=3)
            pe_wide(pe, ph["mlp1_down"], 0, SEQ, 4, (hhi1, hlo1), from_hidden("mlp1_down"))
            pe_wide(pe, ph["a_v"], META, SEQ, 1, (xhi, xlo), from_x(4), norm=4)
            pe.wait_ge(s("av_ssum"), NA + 1)
            for c in range(2):
                mm = nc.tensor.matmul(ps[:, 4, c:c + 1], ssum[:, META + c * P:META + (c + 1) * P], ones[:, 0:1],
                                      start=True, stop=True)
            mm.then_inc(s("av_stat"), 1)
            for g in range(NA // 2):
                c, f = g // 4, g % 4
                if g >= 2:
                    pe.wait_ge(s("av_tok"), g - 1)
                for i in range(4):
                    mm = nc.tensor.transpose(ps[:, 5 + g % 2, i * P:(i + 1) * P],
                                             v_a[:, 4 * f + i, c * P:(c + 1) * P], ident)
                mm.then_inc(s("av_turned"), 1)
            pe.wait_ge(s("av_tok"), 8)
            pe.wait_ge(s("ws_scaled"), 2)
            for f in range(NA):
                if f >= 2:
                    pe.wait_ge(s("sv_done"), f - 1)
                for c in range(2):
                    mm = nc.tensor.matmul(ps[:, 4 + 3 * (f % 2), c * P:(c + 1) * P],
                                          v_atok[:, c, f * P:(f + 1) * P], ws_s[:, c, (f // 2) * P:(f // 2 + 1) * P],
                                          start=True, stop=True)
                mm.then_inc(s("sv_ps"), 1)
            pe_wide(pe, ph["a_u"], META, SEQ, 1, (xhi, xlo), from_x(4))
            pe_wide(pe, ph["a_out"], 0, SEQ, 2, (hhi2, hlo2), from_hidden("a_out"))
            pe_stats(pe, 5, META, SEQ)
            pe_wide(pe, ph["f0_up"], META, SEQ, 1, (xhi, xlo), from_x(5))
            pe_wide(pe, ph["f0_down"], 0, SEQ, 4, (hhi2, hlo2), from_hidden("f0_down"))
            p = ph["b_in"]
            t[0] = 0

            def take_b():
                pe.wait_ge(tile_free, p.tile0 + t[0] - 3)
                t[0] += 1
                return (t[0] - 1) % 4

            def whole_b(k):
                bank = take_b()
                u = p.unit0 + k
                if k == 29:
                    pe.wait_ge(wlo_done, p.unit0 + 32)
                unit(pe, u // UB, u % UB, [(ps[:, bank, 0:SEQ], b == 0, b == 7) for b in range(8)],
                     [x_rhs(b, META, SEQ) for b in range(8)],
                     (lambda b: pe.wait_ge(xlo_done, 8 * 6 + b + 1)) if k == 0 else None)\
                    .then_inc(unit_done, 3 if k == 29 else 1)
            for k in range(NB):
                whole_b(k)
                if k == 1:
                    pe_stats(pe, 6, META, SEQ)
            pe.wait_ge(ulo_done, hid0["b_x"] + NB)
            for hd in range(NB // 2):
                u = p.unit0 + NB + hd
                pe.wait_ge(wlo_done, u + 1)
                for i in range(4):
                    bank = take_b()
                    o = ps[:, bank, 0:SEQ]
                    for kt in range(2):
                        b = 2 * i + kt
                        xh, xl = x_rhs(2 * hd + kt, 0, SEQ, hhi2, hlo2)
                        hi, lo = whi[:, u % HLR, b * P:b * P + P], wlo[:, u % HLR, b * P:b * P + P]
                        nc.tensor.matmul(o, hi, xh, start=kt == 0, stop=False)
                        nc.tensor.matmul(o, hi, xl, start=False, stop=False)
                        mm = nc.tensor.matmul(o, lo, xh, start=False, stop=kt == 1)
                    mm.then_inc(unit_done if i == 3 else s("inner_tile"), 1)
            for k in range(18, 30):
                whole_b(k)
            pe_wide(pe, ph["b_out"], 0, SEQ, 2, (hhi2, hlo2), from_hidden("b_out"))
            pe_stats(pe, 7, META, SEQ)
            pe_wide(pe, ph["f1_up"], META, SEQ, 1, (xhi, xlo), from_x(7))
            pe_wide(pe, ph["f1_down"], 0, SEQ, 4, (hhi2, hlo2), from_hidden("f1_down"))
            pe_stats(pe, 8, META, SEQ)

        @block.vector
        def _(dve):
            dve.wait_ge(small_in, 32)
            dve_log_sigmoid(dve, par("lam", 0, NB), log_lam[:, :], tmp[:, 0, 0:NB], tmp[:, 1, 0:NB],
                            tmp[:, 0, NB:2 * NB], s("lam_step"), s("lam_exp_asked"), s("lam_exp"))
            nc.vector.tensor_scalar(log_lam[:, :], tmp[:, 0, NB:2 * NB], 8.0, None, ALU.mult).then_inc(s("lam_done"), 1)
            for j in range(LA):
                split_lo(dve, 0, j, 8)
            dve.wait_ge(x_loaded, 16)
            for kt in range(KT):
                dve_gain(dve, 0, kt, kt % 2, 0, T0)
            nc.vector.memset(soft[:, :, :, :], 1.0).then_inc(s("soft_set"), 1)
            split_lo(dve, 0, LA, 8)
            dve_rstd(dve, 0, 0, T0)

            p = ph["attn_in"]
            done = [1]

            def to(u):
                while done[0] <= u:
                    j = done[0] % UB
                    ahead(dve, split_lo, p, done[0] // UB, j, done[0] // UB == p.bodies - 1)
                    done[0] += 1

            def head_normed(n):
                _, x, rows, g = QKS[n]
                rr = P if rows == QK else rows
                for k in range(n * HEADS, (n + 1) * HEADS, HEADS):
                    dve.wait_ge(n_root, k + HEADS)
                nc.vector.reciprocal(inv[:, :, :], inv[:, :, :]).then_inc(n_inv, 1)
                dve.wait_ge(n_inv, n + 1)
                nc.vector.scalar_tensor_tensor(out=x[0:rr, :, :], in0=x[0:rr, :, :], scalar=par(g, rows=slice(0, rr)),
                                               in1=inv[0:rr, :, :], op0=ALU.mult, op1=ALU.mult).then_inc(n_out, 1)
                dve.wait_ge(n_out, n + 1)
                if rows == QK:
                    r0 = (n - 2) * 3
                    a, b = slice(64, 96), slice(96, 128)
                    cos = consts[a, K_ROPE:K_ROPE + T0].unsqueeze(1).broadcast_to([32, HEADS, T0])
                    sin = consts[b, K_ROPE:K_ROPE + T0].unsqueeze(1).broadcast_to([32, HEADS, T0])
                    nc.vector.tensor_tensor(x[a, :, :], x[a, :, :], cos, ALU.mult).then_inc(rope_done, 1)
                    nc.vector.tensor_tensor(inv[a, :, :], x[b, :, :], sin, ALU.mult).then_inc(rope_done, 1)
                    dve.wait_ge(rope_done, r0 + 2)
                    nc.vector.tensor_tensor(x[a, :, :], x[a, :, :], inv[a, :, :], ALU.add).then_inc(rope_done, 1)

            for t in range(N_TL):
                u = tile_unit[t]
                to(u)
                if u < 18:
                    dve.wait_ge(unit_done, u + 1)
                else:
                    full = [x for x in range(18, t + 1) if x in (21, 25, 28, 31, 33)]
                    if t in (21, 25, 33):
                        dve.wait_ge(unit_done, u + 1)
                    else:
                        dve.wait_ge(s("inner_tile"), sum(1 for x in range(18, t + 1) if x not in (21, 25, 33)))
                src = ps[:, t % 4, 0:T0]
                if t == 0:
                    nc.vector.tensor_tensor(fg[0:8, 0, :], src[0:8, :], rstd[0:8, :], ALU.mult).then_inc(s("logit"), 1)
                    nc.vector.tensor_tensor(inv[64:128, 0, :], src[64:128, :], rstd[64:128, :],
                                            ALU.mult).then_inc(tile_free, 1)
                elif t < TL_FQ:
                    i = t - TL_CQ
                    nc.vector.tensor_tensor(c_raw[:, i, :], src, rstd[:, :], ALU.mult).then_inc(tile_free, 1)
                    dve.wait_ge(tile_free, t + 1)
                    g = par("g_cq", i) if i < 3 else par("g_ckv", i - 3)
                    if i >= 2:
                        dve.wait_ge(c_lo, i - 1)
                    nc.vector.tensor_scalar(tmp[:, i % 2, :], c_raw[:, i, :], g, None, ALU.mult).then_inc(c_g, 1)
                elif t < TL_FV or TL_KN <= t < TL_V:
                    x, i = (q_fox, t - TL_FQ) if t < TL_FK else (k_fox, t - TL_FK) if t < TL_FV else (k_mla, t - TL_KN)
                    r = rs_c[:, 1, :] if x is k_mla else rstd[:, :]
                    for o in range(2):
                        ins = nc.vector.tensor_tensor(x[0:64, 2 * i + o, :], src[HALF[o], :], r[HALF[o], :], ALU.mult)
                        ins.then_inc(tile_free if o else s("half_tile"), 1)
                elif t < TL_KN:
                    nc.vector.tensor_tensor(v_fm[:, 1, t - TL_FV, :], src, rstd[:, :], ALU.mult).then_inc(tile_free, 1)
                elif t < TL_Q:
                    nc.vector.tensor_tensor(v_fm[:, 0, t - TL_V, :], src, rs_c[:, 1, :], ALU.mult).then_inc(tile_free, 1)
                else:
                    nc.vector.tensor_tensor(q_mla[:, t - TL_Q, :], src, rs_c[:, 0, :], ALU.mult).then_inc(tile_free, 1)
                if t == TL_FQ:
                    dve.wait_ge(s("logit"), 1)
                    nc.vector.tensor_scalar(fg[0:8, 0, :], fg[0:8, 0, :], par("b_forget", rows=slice(0, 8)), None,
                                            ALU.add).then_inc(s("logit"), 1)
                    dve.wait_ge(s("logit"), 2)
                    dve_log_sigmoid(dve, fg[0:8, 0, :], fg[0:8, 1, :], fg[0:8, 2, :], fg[0:8, 3, :], fg[0:8, 4, :],
                                    s("fg_step"), s("fg_exp_asked"), s("fg_exp"))
                    nc.vector.tensor_tensor_scan(fg[0:8, 1, :], ones[0:8, 0:1].broadcast_to([8, T0]), fg[0:8, 4, :],
                                                 0.0, ALU.mult, ALU.add).then_inc(s("fg_sum"), 1)
                    dve.wait_ge(s("fg_sum"), 1)
                if t == TL_FQ + 1:
                    for i in range(2):
                        dve.wait_ge(c_root, i + 1)
                        nc.vector.reciprocal(rs_c[:, i, :], rs_c[:, i, :]).then_inc(c_rstd, 1)
                    dve.wait_ge(c_rstd, 2)
                if t == TL_FV + 1:
                    head_normed(0)
                if t == TL_KN - 1:
                    dve.wait_ge(fox_pad, 2)
                    sel = consts[64:72, K_SEL:K_SEL + HEADS].unsqueeze(2).broadcast_to([8, HEADS, T0])
                    neg = consts[96:104, K_SEL:K_SEL + HEADS].unsqueeze(2).broadcast_to([8, HEADS, T0])
                    f = fg[0:8, 1, :].unsqueeze(1).broadcast_to([8, HEADS, T0])
                    dve.wait_ge(n_out, 1)
                    nc.vector.tensor_scalar(q_fox[64:72, :, :], f, 8.0, None, ALU.mult).then_inc(fox_done, 1)
                    nc.vector.tensor_copy(q_fox[96:104, :, :], neg).then_inc(fox_done, 1)
                    nc.vector.tensor_copy(k_fox[64:72, :, :], sel).then_inc(fox_done, 1)
                    nc.vector.tensor_copy(k_fox[96:104, :, :], f).then_inc(fox_done, 1)
                if t == TL_Q:
                    head_normed(1)
            to(p.units - 1)
            head_normed(2)
            head_normed(3)

            def peak(i):
                b, sf = 4 * (i % 2), soft[:, i % 2, :, :]
                dve.wait_ge(sc_done, i + 1)
                if i >= 2:
                    dve.wait_ge(pn_done, 3 * (i - 1))
                for r, (a, to_, _) in enumerate(SPAN):
                    n = min(P, T0 - a)
                    src = ps[0:n, b, a:a + to_] if r < 2 else ps[0:n, b + 1, 0:to_]
                    nc.vector.tensor_reduce(sf[0:n, 0, r:r + 1], src, AX.X, ALU.max).then_inc(mx_done, 1)
                dve.wait_ge(mx_done, 3 * i + 3)
                nc.vector.tensor_scalar(sf[:, 1, :], sf[:, 0, :], -heads[i][4], None, ALU.mult).then_inc(nb_done, 1)

            def normal(i):
                sf = soft[:, i % 2, :, :]
                dve.wait_ge(ex_done, 3 * i + 3)
                nc.vector.reciprocal(sf[:, 3, :], sf[:, 2, :]).then_inc(rc_done, 1)
                dve.wait_ge(rc_done, i + 1)
                for r, (a, to_, col) in enumerate(SPAN):
                    n = min(P, T0 - a)
                    pr = prob[i % 2][0:n, col:col + to_]
                    nc.vector.tensor_scalar(pr, pr, sf[0:n, 3, r:r + 1], None, ALU.mult).then_inc(pn_done, 1)

            def low(i):
                w, hd = heads[i][5:7]
                rows = HALF[hd % 2]
                dve.wait_ge(ohi_done, i + 1)
                nc.vector.tensor_tensor(clo[rows, 4 * w + hd // 2, :], ps[rows, 4 * (i % 2) + 3, 0:T0],
                                        chi[rows, 4 * w + hd // 2, :].bitcast(F32), ALU.subtract).then_inc(olo_done, 1)
            dve.wait_ge(s("soft_set"), 1)
            for st in range(NHD + 2):
                if st < NHD:
                    peak(st)
                if 1 <= st <= NHD:
                    normal(st - 1)
                if st >= 2:
                    low(st - 2)

            dve_residual(dve, ph["attn_out"], 1, 1, C1, T1)
            dve_rstd(dve, 1, C1, T1, ph["mlp0_up"])
            dve_mlp_up(dve, ph["mlp0_up"], C1, T1)
            dve_residual(dve, ph["mlp0_down"], 4, 2, C1, T1)
            dve_rstd(dve, 2, C1, T1, ph["conv_in"])
            p = ph["conv_in"]
            for it in range(3):
                for j in range(UB):
                    ahead(dve, split_lo, p, it, j, it == 2)
                    k = it * UB + j
                    dve.wait_ge(unit_done, p.unit0 + k + 1)
                    src = ps[:, j % 4, 0:T1]
                    if it == 0:
                        nc.vector.tensor_tensor(gate_c[:, j, :], src, rstd[:, C1:T0], ALU.mult).then_inc(tile_free, 1)
                        continue
                    x = tmp[:, j % 2, 0:T1]
                    nc.vector.tensor_tensor(x, src, rstd[:, C1:T0], ALU.mult).then_inc(tile_free, 1)
                    dve.wait_ge(tile_free, p.tile0 + k + 1)
                    if it == 1:
                        g, y, c = gate_c[:, j, :], conv_y[:, j, :], s("conv_step")
                        nc.vector.tensor_tensor(g, x, g, ALU.mult).then_inc(c, 1)
                        dve.wait_ge(c, 4 * j + 1)
                        nc.vector.tensor_scalar(y, g[:, 0:SEQ], par("conv_w", 3 * j), None, ALU.mult).then_inc(c, 1)
                        for tap in (1, 2):
                            dve.wait_ge(c, 4 * j + 1 + tap)
                            nc.vector.scalar_tensor_tensor(out=y, in0=g[:, tap:tap + SEQ],
                                                           scalar=par("conv_w", 3 * j + tap), in1=y,
                                                           op0=ALU.mult, op1=ALU.add).then_inc(c, 1)
                    else:
                        dve.wait_ge(s("conv_step"), 32)
                        dve.wait_ge(ulo_done, hid0["conv_in"] + j - 1)
                        nc.vector.tensor_tensor(act1[:, j % 2, 0:SEQ], x[:, HALO:T1], conv_y[:, j, :],
                                                ALU.mult).then_inc(u_done, 1)
            dve_residual(dve, ph["conv_out"], 1, 3, META, SEQ)
            dve_rstd(dve, 3, META, SEQ, ph["mlp1_up"])
            dve_mlp_up(dve, ph["mlp1_up"], META, SEQ)
            dve_residual(dve, ph["mlp1_down"], 4, 4, META, SEQ)
            dve_rstd(dve, 4, META, SEQ, ph["a_v"])

            def scaled(p, ready):
                def body(it, last):
                    for j in range(UB):
                        k = it * UB + j
                        dve.wait_ge(unit_done, k + (p.unit0 + 1))
                        if not isinstance(k, int) or k >= 2:
                            dve.wait_ge(ready, k - 1)
                        nc.vector.tensor_tensor(tmp[:, j % 2, 0:SEQ], ps[:, j % 4, 0:SEQ], rstd[:, META:T0],
                                                ALU.mult).then_inc(tile_free, 1)
                        ahead(dve, split_lo, p, it, j, last)
                loop_peeled(dve, p.bodies, body)
            scaled(ph["a_v"], s("av_gelu"))
            dve.wait_ge(s("av_root"), 1)
            nc.vector.reciprocal(root[:, 2:4], root[:, 0:2]).then_inc(s("av_rstd"), 1)
            dve.wait_ge(s("av_rstd"), 1)
            dve.wait_ge(s("ws_masked"), 1)
            for c in range(2):
                nc.vector.tensor_scalar(ws_s[:, c, :], ws[:, :], root[:, 2 + c:3 + c], None,
                                        ALU.mult).then_inc(s("ws_scaled"), 1)
            dve.wait_ge(s("bs_loaded"), 16)
            dve.wait_ge(s("av_tok"), 8)
            for f in range(NA):
                dve.wait_ge(s("sv_ps"), f + 1)
                b3 = bs[:, f // 2, :].unsqueeze(1).broadcast_to([P, 2, P])
                nc.vector.scalar_tensor_tensor(
                    out=v_a[:, f, :].rearrange("p (c n) -> p c n", c=2),
                    in0=ps[:, 4 + 3 * (f % 2), 0:SEQ].rearrange("p (c n) -> p c n", c=2),
                    scalar=par("v_gain", f), in1=b3, op0=ALU.mult, op1=ALU.add).then_inc(s("sv_done"), 1)
            scaled(ph["a_u"], s("au_gelu"))
            dve_residual(dve, ph["a_out"], 2, 5, META, SEQ)
            dve_rstd(dve, 5, META, SEQ)
            dve_pre(dve, 5, META, SEQ)
            dve_ffn_up(dve, ph["f0_up"], 0)
            dve_residual(dve, ph["f0_down"], 4, 6, META, SEQ)
            dve_rstd(dve, 6, META, SEQ, ph["b_in"])

            p = ph["b_in"]
            dve.wait_ge(s("lam_done"), 1)
            for k in range(NB):
                ahead(dve, split_lo, p, k // UB, k % UB, False)
                dve.wait_ge(unit_done, p.unit0 + k + 1)
                x, y = tmp[:, k % 2, 0:SEQ], xb[:, k, :]
                nc.vector.tensor_tensor(x, ps[:, k % 4, 0:SEQ], rstd[:, META:T0], ALU.mult).then_inc(tile_free, 1)
                dve.wait_ge(tile_free, p.tile0 + k + 1)
                c = s("b_conv_step")
                nc.vector.tensor_scalar(y, x, par("b_conv_w", 4 * k + 3), par("b_conv_b", k), ALU.mult,
                                        ALU.add).then_inc(c, 1)
                for tap in (2, 1, 0):
                    o = 3 - tap
                    dve.wait_ge(c, 3 * k + o)
                    ins = nc.vector.scalar_tensor_tensor(out=y[:, o:SEQ], in0=x[:, 0:SEQ - o],
                                                         scalar=par("b_conv_w", 4 * k + tap), in1=y[:, o:SEQ],
                                                         op0=ALU.mult, op1=ALU.add)
                    ins.then_inc(c if tap else u_done, 1)
            for k in range(NB, NB + 6):
                ahead(dve, split_lo, p, k // UB, k % UB, False)
            for k in range(18, 32):
                ahead(dve, split_lo, p, k // UB, k % UB, k // UB == 3)
                if k >= 30:
                    continue
                t = k - 18
                dve.wait_ge(unit_done, p.unit0 + k + (3 if k == 29 else 1))
                nc.vector.tensor_tensor(h_gate(t), ps[:, t % 4, 0:SEQ], rstd[:, META:T0], ALU.mult).then_inc(tile_free, 1)
                dve.wait_ge(s("b_tanh"), t + 1)
                a, th, sq_ = decay[:, t, :], work1[:, t, :], tmp[:, t % 2, 0:SEQ]
                nc.vector.tensor_tensor(sq_, a, a, ALU.mult).then_inc(s("b_aa"), 1)
                dve.wait_ge(s("b_aa"), t + 1)
                nc.vector.scalar_tensor_tensor(out=th, in0=sq_, scalar=1.0, in1=th, op0=ALU.add,
                                               op1=ALU.mult).then_inc(s("b_m2"), 1)
            for t in range(NB):
                bt, a, hs = xb[:, t, :], decay[:, t, :], work1[:, t, :]
                dve.wait_ge(s("b_term"), t + 1)
                nc.vector.tensor_tensor_scan(hs, a, bt, 0.0, ALU.mult, ALU.add).then_inc(s("b_scan"), 1)
            for t in range(NB):
                dve.wait_ge(s("b_scan"), NB)
                dve.wait_ge(s("b_gelu"), t + 1)
                nc.vector.tensor_tensor(xb[:, t, :], work1[:, t, :], h_gate(t), ALU.mult).then_inc(u_done, 1)
            dve_residual(dve, ph["b_out"], 2, 7, META, SEQ)
            dve_rstd(dve, 7, META, SEQ)
            dve_pre(dve, 7, META, SEQ)
            dve_ffn_up(dve, ph["f1_up"], 1)
            dve_residual(dve, ph["f1_down"], 4, 8, META, SEQ)
            dve_rstd(dve, 8, META, SEQ)
            for kt in range(KT):
                hh = h[:, kt, META:T0]
                nc.vector.scalar_tensor_tensor(out=hh, in0=hh, scalar=par("norm_final", kt), in1=rstd[:, META:T0],
                                               op0=ALU.mult, op1=ALU.mult).then_inc(out_ready, 1)

        @block.scalar
        def _(act):
            act.wait_ge(s("lam_exp_asked"), 1)
            nc.scalar.activation(log_lam[:, :], log_lam[:, :], ACT.Exp).then_inc(s("lam_exp"), 1)
            for j in range(LA):
                split_hi(act, 0, j, 8, first=True)
            act.wait_ge(x_loaded, 16)
            for kt in range(KT):
                act_square(act, 0, kt, kt % 2, 0, T0)
                act_xhi(act, 0, kt, kt % 2, 0, T0)
            split_hi(act, 0, LA, 8, first=True)
            act_root(act, 0, 0, T0)

            p = ph["attn_in"]
            done = [1]

            def to(u):
                while done[0] <= u:
                    j = done[0] % UB
                    rnd = done[0] // UB + (j + LA) // UB
                    split_hi(act, rnd, (j + LA) % UB, 8, first=rnd == 0)
                    done[0] += 1

            def roots(n):
                rows = QKS[n][2]
                if n:
                    act.wait_ge(n_out, n)
                if n > 2:
                    act.wait_ge(rope_done, 3)
                for hd in range(HEADS):
                    k = n * HEADS + hd
                    act.wait_ge(n_ss, k + 1)
                    nc.scalar.activation(inv[:, hd, :], ps[:, 6 + k % 2, 0:T0], ACT.Sqrt, scale=1.0 / rows,
                                         bias=par("eps")).then_inc(n_root, 1)

            def squares(n):
                _, x, rows, _ = QKS[n]
                if n:
                    act.wait_ge(n_ss, n * HEADS)
                else:
                    act.wait_ge(c_ss, 2)
                act.wait_ge(tile_free, [TL_FQ + 4, TL_FK + 4, TL_KN + 4, N_TL][n])
                if n == 2:
                    act.wait_ge(kpe_done, 1)
                nc.scalar.activation(wide3[0:rows, :, :], x[0:rows, :, :], ACT.Square).then_inc(n_sq, 1)

            for t in range(N_TL):
                to(tile_unit[t])
                if TL_CQ <= t < TL_FQ:
                    i = t - TL_CQ
                    act.wait_ge(tile_free, t + 1)
                    nc.scalar.activation(wide3[:, i, :], c_raw[:, i, :], ACT.Square).then_inc(c_sq, 1)
                    act.wait_ge(c_g, i + 1)
                    nc.scalar.activation(chi[:, i, :], tmp[:, i % 2, :], ACT.Copy).then_inc(c_hi, 1)
                if t == TL_FQ:
                    act.wait_ge(s("fg_exp_asked"), 1)
                    nc.scalar.activation(fg[0:8, 1, :], fg[0:8, 1, :], ACT.Exp).then_inc(s("fg_exp"), 1)
                if t == TL_FQ:
                    for i in range(2):
                        act.wait_ge(c_ss, i + 1)
                        nc.scalar.activation(rs_c[:, i, :], ps[:, 4 + i, 0:T0], ACT.Sqrt,
                                             scale=1.0 / (384, 256)[i], bias=par("eps")).then_inc(c_root, 1)
                if t == TL_FK:
                    act.wait_ge(kpe_done, 1)
                    squares(0)
                if t == TL_FV:
                    roots(0)
                    squares(1)
                if t == TL_KN:
                    roots(1)
                if t == TL_V:
                    squares(2)
            to(p.units - 1)
            roots(2)
            squares(3)
            for k in range(6):
                w, kt = k // 3, k % 3
                n = min(P, T0 - kt * P)
                act.wait_ge(vt_ps, k + 1)
                nc.scalar.activation(v_tok[0:n, w, kt, :], ps[0:n, 4 + k % 2, :], ACT.Copy).then_inc(vt_done, 1)
            roots(3)

            def exps(i):
                b, sf = 4 * (i % 2), soft[:, i % 2, :, :]
                act.wait_ge(nb_done, i + 1)
                if i >= 2:
                    act.wait_ge(pt_ps, i - 1)
                else:
                    act.wait_ge(n_ss, 4 * HEADS)
                for r, (a, to_, col) in enumerate(SPAN):
                    n = min(P, T0 - a)
                    src = ps[0:n, b, a:a + to_] if r < 2 else ps[0:n, b + 1, 0:to_]
                    nc.scalar.activation(prob[i % 2][0:n, col:col + to_], src, ACT.Exp, bias=sf[0:n, 1, r:r + 1],
                                         scale=heads[i][4], accum_out=sf[0:n, 2, r:r + 1]).then_inc(ex_done, 1)

            def turned(i):
                b = 4 * (i % 2) + 2
                act.wait_ge(pt_ps, i + 1)
                if i >= 2:
                    act.wait_ge(pv_done, i - 1)
                nc.scalar.activation(prob_t[i % 2][:, 0:416], ps[:, b, 0:416], ACT.Copy).then_inc(pt_done, 1)
                nc.scalar.activation(prob_t[i % 2][0:META, 416:432], ps[0:META, b, 416:432],
                                     ACT.Copy).then_inc(pt_done, 1)

            def high(i):
                w, hd = heads[i][5:7]
                rows = HALF[hd % 2]
                act.wait_ge(pv_done, i + 1)
                nc.scalar.activation(chi[rows, 4 * w + hd // 2, :], ps[rows, 4 * (i % 2) + 3, 0:T0],
                                     ACT.Copy).then_inc(ohi_done, 1)
            for st in range(NHD + 2):
                if st < NHD:
                    exps(st)
                if 1 <= st <= NHD:
                    turned(st - 1)
                if st >= 2:
                    high(st - 2)

            act_residual(act, ph["attn_out"], 1, 1, C1, T1)
            act_root(act, 1, C1, T1, ph["mlp0_up"])
            act_hidden(act, ph["mlp0_up"], hhi1, act1, T1)
            act_residual(act, ph["mlp0_down"], 4, 2, C1, T1)
            act_root(act, 2, C1, T1, ph["conv_in"])
            p = ph["conv_in"]
            for it in range(3):
                for j in range(UB):
                    ahead(act, split_hi, p, it, j, it == 2)
                    if it == 2:
                        act.wait_ge(u_done, hid0["conv_in"] + j + 1)
                        nc.scalar.activation(hhi1[:, j, 0:SEQ], act1[:, j % 2, 0:SEQ], ACT.Copy).then_inc(uhi_done, 1)
            act_residual(act, ph["conv_out"], 1, 3, META, SEQ)
            act_root(act, 3, META, SEQ, ph["mlp1_up"])
            act_hidden(act, ph["mlp1_up"], hhi1, act1, SEQ)
            act_residual(act, ph["mlp1_down"], 4, 4, META, SEQ)
            act_root(act, 4, META, SEQ, ph["a_v"])

            act.wait_ge(unit_done, ph["a_v"].unit0)
            act.dma_start(ws[:, :], ws_in).then_inc(s("ws_loaded"), 16)
            act.dma_start(bs[:, :, :], bs_in).then_inc(s("bs_loaded"), 16)
            p = ph["a_v"]

            def body(it, last):
                for j in range(UB):
                    ahead(act, split_hi, p, it, j, last)
                    k = it * UB + j
                    act.wait_ge(tile_free, k + (p.tile0 + 1))
                    nc.scalar.activation(v_a[:, k, :], tmp[:, j % 2, 0:SEQ], ACT.Gelu_apprx_tanh).then_inc(s("av_gelu"), 1)
            loop_peeled(act, p.bodies, body)
            act.wait_ge(s("av_stat"), 1)
            nc.scalar.activation(root[:, 0:2], ps[:, 4, 0:2], ACT.Sqrt, scale=1.0 / (2 * D),
                                 bias=par("eps")).then_inc(s("av_root"), 1)
            for g in range(NA // 2):
                c, f = g // 4, g % 4
                act.wait_ge(s("av_turned"), g + 1)
                nc.scalar.activation(v_atok[:, c, f * 512:(f + 1) * 512], ps[:, 5 + g % 2, :],
                                     ACT.Copy).then_inc(s("av_tok"), 1)
            p2 = ph["a_u"]

            def body_u(it, last):
                for j in range(UB):
                    ahead(act, split_hi, p2, it, j, last)
                    k = it * UB + j
                    act.wait_ge(tile_free, k + (p2.tile0 + 1))
                    act.wait_ge(u_done, k + (hid0["a_u"] - 1))
                    nc.scalar.activation(act2[:, j % 2, :], tmp[:, j % 2, 0:SEQ],
                                         ACT.Gelu_apprx_tanh).then_inc(s("au_gelu"), 1)
                    if k:
                        high_u(k - 1)

            def high_u(k):
                act.wait_ge(u_done, k + (hid0["a_u"] + 1))
                nc.scalar.activation(hhi2[:, k, :], xg[:, k % 2, 0:SEQ], ACT.Copy).then_inc(uhi_done, 1)
            loop_ends(act, p2.bodies, body_u)
            high_u(NA - 1)
            act_residual(act, ph["a_out"], 2, 5, META, SEQ)
            act_root(act, 5, META, SEQ)
            act_pre(act, 5, META, SEQ)
            act_ffn_up(act, ph["f0_up"], 0)
            act_residual(act, ph["f0_down"], 4, 6, META, SEQ)
            act_root(act, 6, META, SEQ, ph["b_in"])

            p = ph["b_in"]
            for k in range(NB):
                ahead(act, split_hi, p, k // UB, k % UB, False)
                act.wait_ge(u_done, hid0["b_x"] + k + 1)
                nc.scalar.activation(hhi2[:, k, :], xb[:, k, :], ACT.Copy).then_inc(uhi_done, 1)
            for hd in range(NB // 2):
                k = NB + hd
                ahead(act, split_hi, p, k // UB, k % UB, False)
                for i in range(4):
                    t = NB + 4 * hd + i
                    if i == 3:
                        act.wait_ge(unit_done, p.unit0 + k + 1)
                    else:
                        act.wait_ge(s("inner_tile"), 3 + 3 + 7 + (3 * hd + i + 1))
                    f = 2 * hd + i % 2
                    if i < 2:
                        nc.scalar.activation(work1[:, f, :], ps[:, t % 4, 0:SEQ], ACT.Sigmoid,
                                             bias=par("b_b_a", f)).then_inc(tile_free, 1)
                    else:
                        if f >= 2:
                            act.wait_ge(s("b_ix"), f - 1)
                        nc.scalar.activation(act2[:, f % 2, :], ps[:, t % 4, 0:SEQ], ACT.Sigmoid,
                                             bias=par("b_b_x", f)).then_inc(tile_free, 1)
            act.wait_ge(tile_free, p.tile0 + 3 * NB)
            act.wait_ge(s("lam_done"), 1)
            for k in range(18, 32):
                ahead(act, split_hi, p, k // UB, k % UB, k // UB == 3)
                t = k - 18
                if k < 30:
                    L = log_lam[:, t:t + 1]
                    nc.scalar.activation(decay[:, t, :], work1[:, t, :], ACT.Exp, scale=L).then_inc(s("b_exp"), 1)
                    act.wait_ge(s("b_exp"), t + 1)
                    nc.scalar.activation(work1[:, t, :], work1[:, t, :], ACT.Tanh, scale=L).then_inc(s("b_tanh"), 1)
            for t in range(NB):
                act.wait_ge(s("b_m2"), t + 1)
                nc.scalar.activation(work1[:, t, :], work1[:, t, :], ACT.Sqrt, scale=-1.0).then_inc(s("b_mult"), 1)
            for t in range(NB):
                act.wait_ge(tile_free, p.tile0 + 3 * NB + t + 1)
                nc.scalar.activation(h_gate(t), h_gate(t), ACT.Gelu_apprx_tanh).then_inc(s("b_gelu"), 1)
            for t in range(NB):
                act.wait_ge(u_done, hid0["b_in"] + t + 1)
                nc.scalar.activation(hhi2[:, t, :], xb[:, t, :], ACT.Copy).then_inc(uhi_done, 1)
            act_residual(act, ph["b_out"], 2, 7, META, SEQ)
            act_root(act, 7, META, SEQ)
            act_pre(act, 7, META, SEQ)
            act_ffn_up(act, ph["f1_up"], 1)
            act_residual(act, ph["f1_down"], 4, 8, META, SEQ)
            act_root(act, 8, META, SEQ)

        @block.gpsimd
        def _(pool):
            pool_clear(pool, 0)
            for kt in range(KT):
                pool_xlo(pool, 0, kt, kt % 2, 0, T0)
                pool_ssum(pool, 0, kt, kt % 2, 0, T0)
            for i in range(5):
                if i == 0:
                    pool.wait_ge(tile_free, 1)
                    src = inv[64:128, 0, :].unsqueeze(1).broadcast_to([64, HEADS, T0])
                    nc.gpsimd.tensor_copy(k_mla[64:128, :, :], src).then_inc(kpe_done, 1)
                    nc.gpsimd.memset(q_fox[64:128, :, :], 0.0).then_inc(fox_pad, 1)
                    nc.gpsimd.memset(k_fox[64:128, :, :], 0.0).then_inc(fox_pad, 1)
                    pool.wait_ge(kpe_done, 1)
                    pool.wait_ge(fox_pad, 2)
                pool.wait_ge(c_hi, i + 1)
                nc.gpsimd.tensor_tensor(clo[:, i, :], tmp[:, i % 2, :], chi[:, i, :].bitcast(F32),
                                        ALU.subtract).then_inc(c_lo, 1)
            pool_residual(pool, ph["attn_out"], 1, 1, C1, T1)
            pool_hidden(pool, ph["mlp0_up"], hhi1, hlo1, act1, T1)
            pool_residual(pool, ph["mlp0_down"], 4, 2, C1, T1)
            for j in range(UB):
                pool.wait_ge(uhi_done, hid0["conv_in"] + j + 1)
                nc.gpsimd.tensor_tensor(hlo1[:, j, 0:SEQ], act1[:, j % 2, 0:SEQ], hhi1[:, j, 0:SEQ].bitcast(F32),
                                        ALU.subtract).then_inc(ulo_done, 1)
            pool_residual(pool, ph["conv_out"], 1, 3, META, SEQ)
            pool_hidden(pool, ph["mlp1_up"], hhi1, hlo1, act1, SEQ)
            pool_residual(pool, ph["mlp1_down"], 4, 4, META, SEQ)
            c = s("av_ssum")
            pool.wait_ge(stat_done, 5)
            nc.gpsimd.memset(ssum[:, :], 0.0).then_inc(c, 1)

            def body(it):
                for j in range(UB):
                    k = it * UB + j
                    pool.wait_ge(s("av_gelu"), k + 1)
                    nc.gpsimd.tensor_tensor(sq[:, j % 2, 0:SEQ], v_a[:, k, :], v_a[:, k, :],
                                            ALU.mult).then_inc(s("av_square"), 1)
                    pool.wait_ge(s("av_square"), k + 1)
                    pool.wait_ge(c, k + 1)
                    nc.gpsimd.tensor_tensor(ssum[:, META:T0], ssum[:, META:T0], sq[:, j % 2, 0:SEQ],
                                            ALU.add).then_inc(c, 1)
            loop(pool, 2, body)
            pool.wait_ge(s("ws_loaded"), 16)
            w3 = ws[:, :].rearrange("p (g t) -> p g t", g=GROUPS)
            nc.gpsimd.affine_select(out=w3, in_=w3, compare_op=ALU.is_ge, fill=0.0, base=0,
                                    pattern=[[0, GROUPS], [1, P]], channel_multiplier=-1).then_inc(s("ws_masked"), 1)
            pool.wait_ge(s("sv_done"), NA)

            def low_u(k):
                pool.wait_ge(uhi_done, k + (hid0["a_u"] + 1))
                nc.gpsimd.tensor_tensor(hlo2[:, k, :], xg[:, k % 2, 0:SEQ], hhi2[:, k, :].bitcast(F32),
                                        ALU.subtract).then_inc(ulo_done, 1)
            for k in range(NA):
                pool.wait_ge(s("au_gelu"), k + 1)
                pool.wait_ge(ulo_done, hid0["a_u"] + k - 1)
                nc.gpsimd.tensor_tensor(xg[:, k % 2, 0:SEQ], act2[:, k % 2, :], v_a[:, k, :],
                                        ALU.mult).then_inc(u_done, 1)
                if k:
                    low_u(k - 1)
            low_u(NA - 1)
            pool.wait_ge(s("av_stat"), 1)
            pool_residual(pool, ph["a_out"], 2, 5, META, SEQ)
            pool_pre(pool, 5, META, SEQ)
            pool_ffn_up(pool, ph["f0_up"], 0)
            pool_residual(pool, ph["f0_down"], 4, 6, META, SEQ)
            for t in range(NB):
                pool.wait_ge(uhi_done, hid0["b_x"] + t + 1)
                nc.gpsimd.tensor_tensor(hlo2[:, t, :], xb[:, t, :], hhi2[:, t, :].bitcast(F32),
                                        ALU.subtract).then_inc(ulo_done, 1)
            tb = ph["b_in"].tile0 + NB
            for t in range(NB):
                pool.wait_ge(tile_free, tb + 4 * (t // 2) + 2 + t % 2 + 1)
                nc.gpsimd.tensor_tensor(xb[:, t, :], xb[:, t, :], act2[:, t % 2, :], ALU.mult).then_inc(s("b_ix"), 1)
            for t in range(NB):
                pool.wait_ge(s("b_mult"), t + 1)
                pool.wait_ge(s("b_ix"), t + 1)
                nc.gpsimd.tensor_tensor(xb[:, t, :], xb[:, t, :], work1[:, t, :], ALU.mult).then_inc(s("b_term"), 1)
            for t in range(NB):
                pool.wait_ge(uhi_done, hid0["b_in"] + t + 1)
                nc.gpsimd.tensor_tensor(hlo2[:, t, :], xb[:, t, :], hhi2[:, t, :].bitcast(F32),
                                        ALU.subtract).then_inc(ulo_done, 1)
            pool_residual(pool, ph["b_out"], 2, 7, META, SEQ)
            pool_pre(pool, 7, META, SEQ)
            pool_ffn_up(pool, ph["f1_up"], 1)
            pool_residual(pool, ph["f1_down"], 4, 8, META, SEQ)


def blocks_of(w):
    k, n = w.shape
    return w.reshape(k // P, P, n // P, P).transpose(0, 2, 1, 3)


def units_by_tile(w, blocks):
    b = blocks_of(w)
    kt, nt = b.shape[:2]
    return b.transpose(1, 0, 2, 3).reshape(nt * kt // blocks, blocks, P, P)


def slabs_of(units):
    u, b = units.shape[:2]
    return units.reshape(u // 2, 2, b, P, P).transpose(0, 3, 1, 2, 4).reshape(u // 2, P, 2 * b * P)


def pad_rows(a):
    return np.concatenate([a, np.zeros((P - a.shape[0],) + a.shape[1:], a.dtype)], 0)


def swapped(w):
    half = ROPE // 2
    nope, r = w[..., :NOPE], w[..., NOPE:]
    return np.concatenate([nope, r, r[..., half:], r[..., :half]], -1)


def lay_out(i):
    z = np.zeros
    f = np.float32
    w_in = i["w_in_attn"][0]
    c_q, c_kv, k_pe, fq, fk, fv, fl = np.split(w_in, np.cumsum([384, 256, 32, 512, 512, 512]), axis=1)
    half = ROPE // 2
    shared = np.concatenate([fl, z((D, NOPE - HEADS), f), k_pe, k_pe[:, half:], k_pe[:, :half]], 1)
    uq = swapped(i["w_uq"][0].reshape(384, HEADS, QK)).reshape(384, HEADS * P)
    ukv = i["w_ukv"][0].reshape(256, HEADS, NOPE + DV)
    k_up, v_up = ukv[..., :NOPE].reshape(256, -1), ukv[..., NOPE:].reshape(256, -1)
    attn = [units_by_tile(np.concatenate([shared, c_q, c_kv, fq, fk, fv], 1), 8),
            units_by_tile(k_up, 8), units_by_tile(v_up, 8), units_by_tile(uq, 8), z((1, 8, P, P), f)]
    gate_b, gate_c, u = np.split(i["w_in_conv"][0], 3, axis=1)

    def pairs(w):
        k, n = w.shape
        return w.reshape(k, 2, n // 2 // P, P).transpose(0, 2, 1, 3).reshape(k, n)
    a_u, a_v = np.split(i["a_w_in_2"][0], 2, axis=1)
    b_g, b_x = np.split(i["b_w_in_2"][0], 2, axis=1)
    wa, wx = i["b_w_a_2"][0], i["b_w_x_2"][0]
    gates = np.stack([np.concatenate([units_by_tile(wa[n], 2), units_by_tile(wx[n], 2)]).reshape(8, P, P)
                      for n in range(6)])
    eight = attn + [units_by_tile(i["w_out_attn"][0], 8),
                    units_by_tile(i["w_mlp_up"][0], 8), units_by_tile(i["w_mlp_down"][0], 8),
                    units_by_tile(np.concatenate([gate_c, u, gate_b], 1), 8), units_by_tile(i["w_out_conv"][0], 8),
                    units_by_tile(i["w_mlp_up"][1], 8), units_by_tile(i["w_mlp_down"][1], 8),
                    units_by_tile(a_v, 8), units_by_tile(a_u, 8), units_by_tile(i["a_w_out_2"][0], 8),
                    units_by_tile(pairs(i["f_w_up_2"][0]), 8),
                    units_by_tile(b_x, 8), gates, units_by_tile(b_g, 8), z((2, 8, P, P), f),
                    units_by_tile(pairs(i["f_w_up_2"][1]), 8)]
    six = [units_by_tile(i["f_w_down_2"][0], 6), units_by_tile(i["b_w_out_2"][0], 6),
           units_by_tile(i["f_w_down_2"][1], 6)]
    w8 = slabs_of(np.concatenate(eight))
    w6 = slabs_of(np.concatenate(six))

    def cols(a):
        a = a.reshape(-1, a.shape[-1])
        k, n = a.shape
        return a.reshape(k, n // P, P).transpose(2, 1, 0).reshape(P, -1)

    def pair_cols(a):
        a = a.reshape(-1, a.shape[-1])
        k, n = a.shape
        return cols(a.reshape(k, 2, n // 2 // P, P).transpose(0, 2, 1, 3).reshape(k, n))
    v = {
        "g_mix0": cols(i["g_mix"][0]), "g_mix1": cols(i["g_mix"][1]), "g_mlp0": cols(i["g_mlp"][0]),
        "g_mlp1": cols(i["g_mlp"][1]), "norm_mix0": cols(i["norm_mix_2"][0]), "norm_mix1": cols(i["norm_mix_2"][1]),
        "norm_ffn0": cols(i["norm_ffn_2"][0]), "norm_ffn1": cols(i["norm_ffn_2"][1]),
        "norm_final": cols(i["norm_final_2"]), "g_cq": cols(i["g_cq"]), "g_ckv": cols(i["g_ckv"]),
        "g_q_mla": swapped(i["g_q_mla"]).T, "g_k_mla": swapped(i["g_k_mla"]).T,
        "g_q_fox": pad_rows(i["g_q_fox"].T), "g_k_fox": pad_rows(i["g_k_fox"].T),
        "b_forget": pad_rows(i["b_forget"].T), "eps": np.full((P, 1), EPS, f), "conv_w": cols(i["conv_w"][0]),
        "v_gain": cols(i["a_v_gain_2"]), "b_conv_w": cols(i["b_conv_w_2"][0]), "b_conv_b": cols(i["b_conv_b_2"]),
        "b_b_a": cols(i["b_b_a_2"].reshape(-1)), "b_b_x": cols(i["b_b_x_2"].reshape(-1)),
        "lam": cols(i["b_lambda_2"]), "f_conv_w0": pair_cols(i["f_conv_w_2"][0]),
        "f_conv_b0": pair_cols(i["f_conv_b_2"][0]), "f_conv_w1": pair_cols(i["f_conv_w_2"][1]),
        "f_conv_b1": pair_cols(i["f_conv_b_2"][1]),
    }
    columns, _ = param_columns()
    assert all(v[n].shape == (P, k) for n, (_, k) in columns.items())
    params = np.concatenate([v[n] for n in columns], 1)

    pos = np.arange(T0, dtype=f)
    inv_freq = (10000.0 ** (-np.arange(0, ROPE, 2) / ROPE)).astype(f)
    ang = (pos[None, :] * inv_freq[:, None]).astype(f)
    cos, sin = np.cos(ang), np.sin(ang)
    consts = z((P, NCONST), f)
    consts[:, K_IDENT:K_IDENT + P] = np.eye(P)
    consts[:, K_MASK:K_MASK + P] = np.triu(np.full((P, P), NEG), 1)
    consts[:, K_ONES:K_ONES + P] = 1
    consts[64:96, K_ROPE:K_ROPE + T0] = np.concatenate([cos, cos])
    consts[96:128, K_ROPE:K_ROPE + T0] = np.concatenate([-sin, sin])
    consts[64:72, K_SEL:] = np.eye(HEADS)
    consts[96:104, K_SEL:] = -8 * np.eye(HEADS)

    x = np.concatenate([i["meta_tokens"], i["x"][0]], 0)
    return {
        "x_fm": x.T.reshape(KT, P, T0).transpose(1, 0, 2), "w8": w8, "w6": w6, "params_cols": params,
        "constants": consts, "ws_src": i["a_w_s_2"][0].transpose(2, 0, 1).reshape(P, GROUPS * P),
        "bs_rows": np.repeat(i["a_b_s_2"], P, axis=0),
    }


def kernel(**inputs):
    import concourse.bacc as bacc
    from concourse.bass_utils import run_bass_kernel_spmd

    nc = bacc.Bacc("TRN2", target_bir_lowering=False, num_devices=1)
    arrays = {n: np.ascontiguousarray(a) for n, a in lay_out({k: np.asarray(v) for k, v in inputs.items()}).items()}
    args = [nc.dram_tensor(n, a.shape, mybir.dt.from_np(a.dtype), kind="ExternalInput").ap()
            for n, a in arrays.items()]
    args.append(nc.dram_tensor("out_fm", (P, KT, SEQ), F32, kind="ExternalOutput").ap())
    program(nc, *args)
    r = run_bass_kernel_spmd(nc, [arrays], core_ids=[0])
    got = r.results[0]["out_fm"]
    return got.transpose(1, 0, 2).reshape(D, SEQ).T.reshape(1, SEQ, D)
```

```python
from contextlib import ExitStack

import numpy as np

import concourse.bass as bass
from concourse import mybir

F32 = mybir.dt.float32
F32R = mybir.dt.float32r
ACT = mybir.ActivationFunctionType
ALU = mybir.AluOpType
AX = mybir.AxisListType

P = 128
D = 1024
SEQ = 256
META = 16
T0 = SEQ + META
HALO = 2
C1 = META - HALO
T1 = T0 - C1
KT = D // P
HEADS = 8
NOPE, ROPE, QK, DV = 64, 32, 96, 64
FOX_K = 104
EPS = 1e-6
NEG = -1e30
NH1 = 4 * D // P
NH2 = 3 * D // P
NA = 2 * D // P
NB = 3 * D // 2 // P
GROUPS = 8

UB = 8
HLR = 4
RAW = 4
LA = 3

PHASES = [
    ("attn_in", 24, 8, 34), ("attn_out", 8, 8, 8), ("mlp0_up", 32, 8, 32), ("mlp0_down", 32, 8, 8),
    ("conv_in", 24, 8, 24), ("conv_out", 8, 8, 8), ("mlp1_up", 32, 8, 32), ("mlp1_down", 32, 8, 8),
    ("a_v", 16, 8, 16), ("a_u", 16, 8, 16), ("a_out", 16, 8, 8),
    ("f0_up", 48, 8, 48), ("f0_down", 32, 6, 8),
    ("b_in", 32, 8, 48), ("b_out", 16, 6, 8),
    ("f1_up", 48, 8, 48), ("f1_down", 32, 6, 8),
]


class Phase:

    def __init__(self, n, units, blocks, tiles, unit0, tile0):
        self.name, self.units, self.blocks, self.tiles = n, units, blocks, tiles
        self.unit0, self.tile0 = unit0, tile0
        self.bodies = units // UB
        self.next = None


def plan():
    out, u, t = {}, 0, 0
    last = None
    for name, units, blocks, tiles in PHASES:
        ph = Phase(name, units, blocks, tiles, u, t)
        if last:
            last.next = ph
        out[name] = last = ph
        u, t = u + units, t + tiles
    return out


def param_columns():
    sizes = [("g_mix0", 8), ("g_mlp0", 8), ("g_mix1", 8), ("g_mlp1", 8), ("norm_mix0", 8), ("norm_ffn0", 8),
             ("norm_mix1", 8), ("norm_ffn1", 8), ("norm_final", 8), ("g_cq", 3), ("g_ckv", 2), ("g_q_mla", 1),
             ("g_k_mla", 1), ("g_q_fox", 1), ("g_k_fox", 1), ("b_forget", 1), ("eps", 1), ("conv_w", 24),
             ("v_gain", NA), ("b_conv_w", 4 * NB), ("b_conv_b", NB), ("b_b_a", NB), ("b_b_x", NB),
             ("lam", NB), ("f_conv_w0", 3 * 2 * NH2), ("f_conv_b0", 2 * NH2), ("f_conv_w1", 3 * 2 * NH2),
             ("f_conv_b1", 2 * NH2)]
    at, out = 0, {}
    for n, k in sizes:
        out[n] = (at, k)
        at += k
    return out, at


NORM_GAIN = ["g_mix0", "g_mlp0", "g_mix1", "g_mlp1", "norm_mix0", "norm_ffn0", "norm_mix1", "norm_ffn1",
             "norm_final"]
K_IDENT, K_MASK, K_ONES, K_ROPE = 0, P, 2 * P, 3 * P
K_SEL = K_ROPE + T0
NCONST = K_SEL + HEADS * HEADS
ATANH = [1.0 / 15, 1.0 / 13, 1.0 / 11, 1.0 / 9, 1.0 / 7, 1.0 / 5, 1.0 / 3]


def program(nc, x_in, w8, w6, params_in, consts_in, rows_in, pad_in, ws_in, bs_in, out):
    ph = plan()
    pcol, npar = param_columns()
    ctx = ExitStack()
    with ctx:
        def sem(name):
            return ctx.enter_context(nc.semaphore(name))

        def keep(name, shape, dt=F32):
            return ctx.enter_context(nc.sbuf_tensor(name, shape, dt))

        raw = keep("raw", [P, RAW, 2 * UB * P])
        whi = keep("whi", [P, HLR, UB * P], F32R)
        wlo = keep("wlo", [P, HLR, UB * P], F32R)
        h = keep("h", [P, KT, T0])
        xhi = keep("xhi", [P, KT, T0], F32R)
        xlo = keep("xlo", [P, KT, T0], F32R)
        params = keep("params", [P, npar])
        consts = keep("consts", [P, NCONST])
        rstd = keep("rstd", [P, T0])
        root = keep("root", [P, T0])
        ssum = keep("ssum", [P, T0])
        sq = keep("sq", [P, 2, T0])
        xg = keep("xg", [P, 2, T0])
        tmp = keep("tmp", [P, 2, T0])
        log_lam = keep("log_lam", [P, NB])

        with ExitStack() as a:
            def part(name, shape, dt=F32):
                return a.enter_context(nc.sbuf_tensor(name, shape, dt))
            chi = part("chi", [P, KT, T0], F32R)
            clo = part("clo", [P, KT, T0], F32R)
            q_mla = part("q_mla", [P, HEADS, T0])
            k_mla = part("k_mla", [P, HEADS, T0])
            q_fox = part("q_fox", [P, HEADS, T0])
            k_fox = part("k_fox", [P, HEADS, T0])
            v_fm = part("v_fm", [P, 2, 4, T0])
            v_tok = part("v_tok", [P, 2, 3, 4 * P])
            wide = part("wide", [P, HEADS * T0])
            extra = part("extra", [P, HEADS, T0])
            rs_c = part("rs_c", [P, 2, T0])
            rms = part("rms", [HEADS, 2, T0])
            sel_rows = part("sel_rows", [HEADS, HEADS, P])
            fg = part("fg", [P, 5, T0])
            soft = part("soft", [P, 2, 4, 3])
        with ExitStack() as a:
            hhi1 = a.enter_context(nc.sbuf_tensor("hhi1", [P, NH1, T1], F32R))
            hlo1 = a.enter_context(nc.sbuf_tensor("hlo1", [P, NH1, T1], F32R))
            act1 = a.enter_context(nc.sbuf_tensor("act1", [P, 2, T1], F32))
            gate_c = a.enter_context(nc.sbuf_tensor("gate_c", [P, KT, T1], F32))
            conv_y = a.enter_context(nc.sbuf_tensor("conv_y", [P, KT, SEQ], F32))
        with ExitStack() as a:
            hhi2 = a.enter_context(nc.sbuf_tensor("hhi2", [P, NH2, SEQ], F32R))
            hlo2 = a.enter_context(nc.sbuf_tensor("hlo2", [P, NH2, SEQ], F32R))
            act2 = a.enter_context(nc.sbuf_tensor("act2", [P, 2, SEQ], F32))
            work1 = a.enter_context(nc.sbuf_tensor("work1", [P, NA, SEQ], F32))
            work2 = a.enter_context(nc.sbuf_tensor("work2", [P, NA * SEQ], F32))
            ws = a.enter_context(nc.sbuf_tensor("ws", [P, GROUPS * P], F32))
            bs = a.enter_context(nc.sbuf_tensor("bs", [P, GROUPS, P], F32))
            work3 = a.enter_context(nc.sbuf_tensor("work3", [P, NB * SEQ], F32))
        c_raw, k_pe, turned = extra[:, 0:5, :], extra[:, 5, :], extra
        v_a, v_atok = work1, work2[:, :].rearrange("p (c n) -> p c n", c=2)
        ws_s = work3[:, 0:2 * GROUPS * P].rearrange("p (c n) -> p c n", c=2)
        xb = work2[:, 0:NB * SEQ].rearrange("p (t n) -> p t n", t=NB)
        decay = work3[:, :].rearrange("p (t n) -> p t n", t=NB)

        def h_gate(t):
            if t < 4:
                return work1[:, NB + t, :]
            if t < 8:
                return work2[:, (NB + t - 4) * SEQ:(NB + t - 3) * SEQ]
            return ws[:, (t - 8) * SEQ:(t - 7) * SEQ]
        cb = work3[:, 0:4 * SEQ].rearrange("p (t n) -> p t n", t=4)
        gg = work3[:, 4 * SEQ:6 * SEQ].rearrange("p (t n) -> p t n", t=2)
        half = work3[:, 6 * SEQ:8 * SEQ].rearrange("p (t n) -> p t n", t=2)

        ps = ctx.enter_context(nc.psum_tensor("ps", [P, 8, 512], F32))

        ident = consts[:, K_IDENT:K_IDENT + P]
        mask = consts[:, K_MASK:K_MASK + P]
        ones = consts[:, K_ONES:K_ONES + P]

        def par(name, i=0, n=1, rows=slice(0, P)):
            a, _ = pcol[name]
            if isinstance(i, int):
                return params[rows, a + i:a + i + n]
            return params[rows, bass.ds(i + a, n)]

        small_in = sem("small_in")
        consts_in_done = sem("consts_in_done")
        rows_loaded = sem("rows_loaded")
        x_loaded = sem("x_loaded")
        raw_full = [sem(f"raw_full{i}") for i in range(RAW)]
        whi_done = sem("whi_done")
        wlo_done = sem("wlo_done")
        unit_done = sem("unit_done")
        tile_free = sem("tile_free")
        xg_done = sem("xg_done")
        xhi_done = sem("xhi_done")
        xlo_done = sem("xlo_done")
        sq_done = sem("sq_done")
        ssum_done = sem("ssum_done")
        stat_done = sem("stat_done")
        root_done = sem("root_done")
        rstd_done = sem("rstd_done")
        u_done = sem("u_done")
        uhi_done = sem("uhi_done")
        ulo_done = sem("ulo_done")
        out_done = sem("out_done")
        out_ready = sem("out_ready")
        S = {}

        def s(name):
            if name not in S:
                S[name] = sem(name)
            return S[name]

        hid0, at = {}, 0
        for name, n in (("mlp0_up", NH1), ("conv_in", KT), ("mlp1_up", NH1), ("a_u", NA), ("f0_up", NH2),
                        ("b_x", NB), ("b_in", NB), ("f1_up", NH2)):
            hid0[name] = at
            at += n
        made = {"mlp0_down": hid0["mlp0_up"], "conv_out": hid0["conv_in"], "mlp1_down": hid0["mlp1_up"],
                "a_out": hid0["a_u"], "f0_down": hid0["f0_up"], "b_out": hid0["b_in"], "f1_down": hid0["f1_up"]}

        def loop(eng, n, body):
            if n > 1:
                with eng.Fori(0, n) as i:
                    body(i)
            else:
                body(0)

        def loop_ends(eng, n, body):
            body(0, False)
            if n > 3:
                with eng.Fori(1, n - 1) as i:
                    body(i, False)
            elif n == 3:
                body(1, False)
            body(n - 1, True)

        def loop_peeled(eng, n, body):
            if n > 2:
                with eng.Fori(0, n - 1) as i:
                    body(i, False)
            elif n == 2:
                body(0, False)
            body(n - 1, True)

        def split_hi(act, rnd, j, blocks, first=False):
            slot, col, n = (j // 2) % RAW, (j % 2) * blocks * P, blocks * P
            act.wait_ge(raw_full[slot], rnd * 16 + 16)
            if not (first and j < HLR):
                act.wait_ge(unit_done, rnd * UB + (j - HLR + 1))
            nc.scalar.activation(whi[:, j % HLR, 0:n], raw[:, slot, col:col + n], ACT.Copy).then_inc(whi_done, 1)

        def split_lo(dve, rnd, j, blocks):
            slot, col, n = (j // 2) % RAW, (j % 2) * blocks * P, blocks * P
            dve.wait_ge(whi_done, rnd * UB + (j + 1))
            nc.vector.tensor_tensor(wlo[:, j % HLR, 0:n], raw[:, slot, col:col + n],
                                    whi[:, j % HLR, 0:n].bitcast(F32), ALU.subtract).then_inc(wlo_done, 1)

        def ahead(eng, fn, p, it, j, last):
            if p.name in EARLY and isinstance(it, int) and it == j == 0:
                return
            split_ahead(eng, fn, p, it, j, last)

        def split_ahead(eng, fn, p, it, j, last):
            rnd = it + (p.unit0 // UB + (j + LA) // UB)
            blocks = p.blocks
            if last and j + LA >= UB:
                if p.next is None:
                    return
                blocks = p.next.blocks
            fn(eng, rnd, (j + LA) % UB, blocks)

        EARLY = ("attn_in", "mlp0_up", "conv_in", "mlp1_up", "a_v", "b_in")

        def unit(pe, rnd, j, outs, rhs, need=None):
            pe.wait_ge(wlo_done, rnd * UB + (j + 1))
            for b, ((o, start, stop), (xh, xl)) in enumerate(zip(outs, rhs)):
                if need:
                    need(b)
                m = o.shape[0]
                hi = whi[:, j % HLR, b * P:b * P + m]
                lo = wlo[:, j % HLR, b * P:b * P + m]
                nc.tensor.matmul(o, hi, xh, start=start, stop=False)
                nc.tensor.matmul(o, hi, xl, start=False, stop=False)
                mm = nc.tensor.matmul(o, lo, xh, start=False, stop=stop)
            return mm

        def x_rhs(kt, c0, t, hi=xhi, lo=xlo):
            return hi[:, kt, c0:c0 + t], lo[:, kt, c0:c0 + t]

        def pe_wide(pe, p, c0, t, segs, src, made_by, norm=None, after_attention=False):
            per = UB // segs
            ring = 4 if per >= 4 else 2
            ready, base, step = made_by

            def body(it, first):
                rnd = it + p.unit0 // UB
                for j in range(UB):
                    seg, jt = j % segs, j // segs
                    bank = jt % ring + (4 - ring)
                    if seg == 0 and not (after_attention and jt < 4):
                        pe.wait_ge(tile_free, it * per + (p.tile0 + jt - ring + 1))
                    o = ps[:, bank, 0:t]
                    outs = [(o, seg == 0 and b == 0, seg == segs - 1 and b == p.blocks - 1)
                            for b in range(p.blocks)]
                    rhs = [x_rhs(seg * p.blocks + b, c0, t, *src) for b in range(p.blocks)]
                    need = None
                    if first and jt == 0:
                        def need(b, seg=seg):
                            pe.wait_ge(ready, base + step * (seg * p.blocks + b + 1))
                    unit(pe, rnd, j, outs, rhs, need).then_inc(unit_done, 1)
                    if first and norm is not None and j == 1:
                        pe_stats(pe, norm, c0, t)
            body(0, True)
            if p.bodies > 1:
                with pe.Fori(1, p.bodies) as i:
                    body(i, False)

        def pe_stats(pe, n, c0, t):
            pe.wait_ge(ssum_done, 9 * n + 9)
            nc.tensor.matmul(ps[:, 4, 0:t], ones, ssum[:, c0:c0 + t], start=True, stop=True).then_inc(stat_done, 1)

        def from_x(n):
            return xlo_done, 8 * n, 1

        def from_hidden(name):
            return ulo_done, made[name], 1

        PRE = (5, 7)

        def act_root(act, n, c0, t, p=None):
            if p:
                split_ahead(act, split_hi, p, 0, 0, False)
            act.wait_ge(stat_done, n + 1)
            nc.scalar.activation(root[:, c0:c0 + t], ps[:, 4, 0:t], ACT.Sqrt, scale=1.0 / D,
                                 bias=par("eps")).then_inc(root_done, 1)

        def dve_rstd(dve, n, c0, t, p=None):
            if p:
                split_ahead(dve, split_lo, p, 0, 0, False)
            dve.wait_ge(root_done, n + 1)
            nc.vector.reciprocal(rstd[:, c0:c0 + t], root[:, c0:c0 + t]).then_inc(rstd_done, 1)
            dve.wait_ge(rstd_done, n + 1)

        def ring2(kt, even):
            return kt % 2 if isinstance(kt, int) else even

        def dve_gain(dve, n, kt, slot, c0, t):
            if not isinstance(kt, int) or 8 * n + kt >= 2:
                dve.wait_ge(xlo_done, kt + (8 * n - 1))
            nc.vector.tensor_scalar(xg[:, slot, 0:t], h[:, kt, c0:c0 + t], par(NORM_GAIN[n], kt), None,
                                    ALU.mult).then_inc(xg_done, 1)

        def act_square(act, n, kt, slot, c0, t):
            if not isinstance(kt, int) or 8 * n + kt >= 2:
                act.wait_ge(ssum_done, kt + (9 * n))
            nc.scalar.activation(sq[:, slot, 0:t], h[:, kt, c0:c0 + t], ACT.Square).then_inc(sq_done, 1)

        def act_xhi(act, n, kt, slot, c0, t):
            act.wait_ge(xg_done, kt + (8 * n + 1))
            nc.scalar.activation(xhi[:, kt, c0:c0 + t], xg[:, slot, 0:t], ACT.Copy).then_inc(xhi_done, 1)

        def pool_clear(pool, n):
            if n:
                pool.wait_ge(stat_done, n)
            nc.gpsimd.memset(ssum[:, :], 0.0).then_inc(ssum_done, 1)

        def pool_xlo(pool, n, kt, slot, c0, t):
            pool.wait_ge(xhi_done, kt + (8 * n + 1))
            nc.gpsimd.tensor_tensor(xlo[:, kt, c0:c0 + t], xg[:, slot, 0:t],
                                    xhi[:, kt, c0:c0 + t].bitcast(F32), ALU.subtract).then_inc(xlo_done, 1)

        def pool_ssum(pool, n, kt, slot, c0, t):
            pool.wait_ge(sq_done, kt + (8 * n + 1))
            pool.wait_ge(ssum_done, kt + (9 * n + 1))
            nc.gpsimd.tensor_tensor(ssum[:, c0:c0 + t], ssum[:, c0:c0 + t], sq[:, slot, 0:t],
                                    ALU.add).then_inc(ssum_done, 1)

        POST = [n for n in range(9) if n not in PRE and n != 8]

        def dve_residual(dve, p, segs, n, c0, t):
            per = UB // segs
            ring = 4 if per >= 4 else 2

            def body(it, last):
                for j in range(UB):
                    if j % segs != segs - 1:
                        ahead(dve, split_lo, p, it, j, last)
                    if j % segs == segs - 1:
                        jt = j // segs
                        kt = it * per + jt
                        dve.wait_ge(unit_done, it * UB + (p.unit0 + j + 1))
                        hh = h[:, kt, c0:c0 + t]
                        nc.vector.tensor_tensor(hh, ps[:, jt % ring + (4 - ring), 0:t], hh,
                                                ALU.add).then_inc(tile_free, 1)
                        if n in POST:
                            dve.wait_ge(tile_free, kt + (p.tile0 + 1))
                            dve_gain(dve, n, kt, jt % 2, c0, t)
                        ahead(dve, split_lo, p, it, j, last)
            loop_peeled(dve, p.bodies, body)

        def act_residual(act, p, segs, n, c0, t):
            per = UB // segs

            def body(it, last):
                for j in range(UB):
                    ahead(act, split_hi, p, it, j, last)
                    if j % segs == segs - 1:
                        jt = j // segs
                        kt = it * per + jt
                        act.wait_ge(tile_free, kt + (p.tile0 + 1))
                        if n in POST:
                            act_xhi(act, n, kt, jt % 2, c0, t)
                        act_square(act, n, kt, jt % 2, c0, t)
            loop_peeled(act, p.bodies, body)

        def pool_residual(pool, p, segs, n, c0, t):
            per = UB // segs
            pool_clear(pool, n)

            def body(it):
                for jt in range(per):
                    kt = it * per + jt
                    if n in POST:
                        pool_xlo(pool, n, kt, jt % 2, c0, t)
                    pool_ssum(pool, n, kt, jt % 2, c0, t)
            loop(pool, p.bodies, body)

        def dve_pre(dve, n, c0, t):
            for kt in range(KT):
                dve.wait_ge(xlo_done, 8 * n + kt - 1)
                nc.vector.scalar_tensor_tensor(out=xg[:, kt % 2, 0:t], in0=h[:, kt, c0:c0 + t],
                                               scalar=par(NORM_GAIN[n], kt), in1=rstd[:, c0:c0 + t],
                                               op0=ALU.mult, op1=ALU.mult).then_inc(xg_done, 1)

        def act_pre(act, n, c0, t):
            for kt in range(KT):
                act_xhi(act, n, kt, kt % 2, c0, t)

        def pool_pre(pool, n, c0, t):
            for kt in range(KT):
                pool_xlo(pool, n, kt, kt % 2, c0, t)

        def dve_mlp_up(dve, p, c0, t):
            def body(it, last):
                for j in range(UB):
                    k = it * UB + j
                    dve.wait_ge(unit_done, k + (p.unit0 + 1))
                    nc.vector.tensor_tensor(tmp[:, j % 2, 0:t], ps[:, j % 4, 0:t], rstd[:, c0:c0 + t],
                                            ALU.mult).then_inc(tile_free, 1)
                    dve.wait_ge(tile_free, k + (p.tile0 + 1))
                    if p.name != "mlp0_up" or not isinstance(it, int):
                        dve.wait_ge(ulo_done, k + (hid0[p.name] - 1))
                    elif k >= 2:
                        dve.wait_ge(ulo_done, k - 1)
                    nc.vector.scalar_tensor_tensor(out=act1[:, j % 2, 0:t], in0=tmp[:, j % 2, 0:t], scalar=0.0,
                                                   in1=tmp[:, j % 2, 0:t], op0=ALU.max,
                                                   op1=ALU.mult).then_inc(u_done, 1)
                    ahead(dve, split_lo, p, it, j, last)
            loop_ends(dve, p.bodies, body)

        def act_hidden(act, p, hi, src, t):
            def body(it, last):
                for j in range(UB):
                    ahead(act, split_hi, p, it, j, last)
                    k = it * UB + j
                    act.wait_ge(u_done, k + (hid0[p.name] + 1))
                    nc.scalar.activation(hi[:, k, 0:t], src[:, j % 2, 0:t], ACT.Copy).then_inc(uhi_done, 1)
            loop_ends(act, p.bodies, body)

        def pool_hidden(pool, p, hi, lo, src, t):
            def body(it):
                for j in range(UB):
                    k = it * UB + j
                    pool.wait_ge(uhi_done, k + (hid0[p.name] + 1))
                    nc.gpsimd.tensor_tensor(lo[:, k, 0:t], src[:, j % 2, 0:t], hi[:, k, 0:t].bitcast(F32),
                                            ALU.subtract).then_inc(ulo_done, 1)
            loop(pool, p.bodies, body)

        def dve_ffn_up(dve, p, layer):
            pairs = UB // 2
            conv, full = s(f"ffn{layer}_first_tap"), s(f"ffn{layer}_second_tap")

            def body(it, last):
                for j in range(UB):
                    k = it * UB + j
                    w = par(f"f_conv_w{layer}", it * (3 * UB) + 3 * j + 1)
                    w0 = par(f"f_conv_w{layer}", it * (3 * UB) + 3 * j)
                    c = cb[:, j % 4, :]
                    dve.wait_ge(conv, k + 1)
                    nc.vector.scalar_tensor_tensor(out=c[:, 1:SEQ], in0=ps[:, j % 4, 0:SEQ - 1], scalar=w,
                                                   in1=c[:, 1:SEQ], op0=ALU.mult, op1=ALU.add).then_inc(full, 1)
                    dve.wait_ge(full, k + 1)
                    nc.vector.scalar_tensor_tensor(out=c[:, 2:SEQ], in0=ps[:, j % 4, 0:SEQ - 2], scalar=w0,
                                                   in1=c[:, 2:SEQ], op0=ALU.mult,
                                                   op1=ALU.add).then_inc(tile_free, 1)
                    ahead(dve, split_lo, p, it, j, last)
            loop_peeled(dve, p.bodies, body)

        def act_ffn_up(act, p, layer):
            pairs = UB // 2
            conv, gated = s(f"ffn{layer}_first_tap"), s(f"ffn{layer}_gelu")

            def body(it, last):
                for j in range(UB):
                    ahead(act, split_hi, p, it, j, last)
                    k = it * UB + j
                    act.wait_ge(unit_done, k + (p.unit0 + 1))
                    if p.name != "f0_up" or not isinstance(it, int) or it * pairs + j // 2 >= 2:
                        act.wait_ge(u_done, it * pairs + (hid0[p.name] + j // 2 - 1))
                    nc.scalar.activation(cb[:, j % 4, :], ps[:, j % 4, 0:SEQ], ACT.Identity,
                                         scale=par(f"f_conv_w{layer}", it * (3 * UB) + 3 * j + 2),
                                         bias=par(f"f_conv_b{layer}", k)).then_inc(conv, 1)
                    if j % 2 == 0:
                        continue
                    pr = it * pairs + j // 2
                    act.wait_ge(tile_free, k + (p.tile0 + 0))
                    nc.scalar.activation(gg[:, (j // 2) % 2, :], cb[:, (j - 1) % 4, :],
                                         ACT.Gelu_apprx_tanh).then_inc(gated, 1)
                    if not isinstance(pr, int) or pr:
                        high(pr - 1, (j // 2 + 1) % 2)

            def high(pr, slot):
                act.wait_ge(u_done, pr + (hid0[p.name] + 1))
                nc.scalar.activation(hhi2[:, pr, :], half[:, slot, :], ACT.Copy).then_inc(uhi_done, 1)
            loop_ends(act, p.bodies, body)
            high(NH2 - 1, (NH2 - 1) % 2)

        def pool_ffn_up(pool, p, layer):
            pairs = UB // 2
            gated = s(f"ffn{layer}_gelu")

            def low(pr, slot):
                pool.wait_ge(uhi_done, pr + (hid0[p.name] + 1))
                nc.gpsimd.tensor_tensor(hlo2[:, pr, :], half[:, slot, :], hhi2[:, pr, :].bitcast(F32),
                                        ALU.subtract).then_inc(ulo_done, 1)

            def body(it, last):
                for i in range(pairs):
                    pr = it * pairs + i
                    pool.wait_ge(gated, pr + 1)
                    pool.wait_ge(ulo_done, pr + (hid0[p.name] - 1))
                    pool.wait_ge(tile_free, it * UB + (p.tile0 + 2 * i + 2))
                    nc.gpsimd.tensor_tensor(half[:, i % 2, :], gg[:, i % 2, :], cb[:, (2 * i + 1) % 4, :],
                                            ALU.mult).then_inc(u_done, 1)
                    if not isinstance(pr, int) or pr:
                        low(pr - 1, (i + 1) % 2)
            loop_ends(pool, p.bodies, body)
            low(NH2 - 1, (NH2 - 1) % 2)

        def dve_log_sigmoid(dve, z, e, t1, t2, res, done, exp_asked, exp_done):
            n = [0]

            def step(ins):
                n[0] += 1
                ins.then_inc(done, 1)
                dve.wait_ge(done, n[0])
            step(nc.vector.scalar_tensor_tensor(out=t1, in0=z, scalar=-1.0, in1=z, op0=ALU.mult, op1=ALU.min))
            nc.vector.tensor_copy(e, t1).then_inc(exp_asked, 1)
            dve.wait_ge(exp_done, 1)
            step(nc.vector.tensor_scalar(t1, e, 2.0, None, ALU.add))
            step(nc.vector.reciprocal(t1, t1))
            step(nc.vector.tensor_tensor(e, e, t1, ALU.mult))
            step(nc.vector.tensor_tensor(t1, e, e, ALU.mult))
            step(nc.vector.tensor_scalar(t2, t1, ATANH[0], None, ALU.mult))
            for c in ATANH[1:]:
                step(nc.vector.scalar_tensor_tensor(out=t2, in0=t2, scalar=c, in1=t1, op0=ALU.add, op1=ALU.mult))
            step(nc.vector.scalar_tensor_tensor(out=t2, in0=t2, scalar=1.0, in1=e, op0=ALU.add, op1=ALU.mult))
            step(nc.vector.tensor_scalar(t1, z, 0.0, None, ALU.min))
            step(nc.vector.scalar_tensor_tensor(out=res, in0=t2, scalar=-2.0, in1=t1, op0=ALU.mult, op1=ALU.add))

        QKS = [
            ("fq", q_fox, NOPE, "g_q_fox"), ("fk", k_fox, NOPE, "g_k_fox"),
            ("k", k_mla, QK, "g_k_mla"), ("q", q_mla, QK, "g_q_mla")]
        U_PE, U_CQ, U_CKV, U_FQ, U_FK, U_FV, U_KN, U_V, U_Q = 0, 1, 4, 6, 10, 14, 18, 19, 20
        TL_CQ, TL_CKV, TL_FQ, TL_FK, TL_FV, TL_KN, TL_V, TL_Q = 1, 4, 6, 10, 14, 18, 22, 26
        N_TL = 34
        tile_unit = (list(range(18)) + [U_KN] * 4 + [U_V] * 4 + [U_Q + (3 * hd + 2) // 8 for hd in range(HEADS)])
        flat = v_fm[:, :, :, :].rearrange("p w h n -> p (w h n)")
        NPR = P + 2 * P + T0
        NPT = 3 * T0 - 3 * P
        prob = [wide[:, 0:NPR], wide[:, NPR:2 * NPR], flat[:, 0:NPR]]
        prob_t = [wide[:, 2 * NPR + i * NPT:2 * NPR + (i + 1) * NPT] for i in range(2)]
        wide3 = wide[:, :].rearrange("p (h n) -> p h n", h=HEADS)
        c_ss, c_root, c_rstd = s("latent_stat"), s("latent_root"), s("latent_rstd")
        c_sq, c_g, c_hi, c_lo = s("latent_square"), s("latent_gain"), s("latent_hi"), s("latent_lo")
        n_ss, n_root, n_inv, n_sp, n_out = (s("head_stat"), s("head_root"), s("head_inverse"), s("head_spread"),
                                            s("head_normed"))
        n_sq = [s(f"head_square{n}") for n in range(4)]
        rope_cos, rope_sin, rope_done, kpe_done = s("rope_cos"), s("rope_sin"), s("rope_done"), s("kpe_copied")
        pad_done = s("pad_loaded")
        vt_ps, vt_done = s("v_turned"), s("v_tok_done")
        fox_done = s("fox_rows_done")
        sc_done, mx_done, nb_done, ex_done = s("scores_done"), s("max_done"), s("minus_max"), s("exp_done")
        rc_done, pn_done, pt_ps, pt_done = s("sum_inverse"), s("prob_done"), s("prob_turned"), s("prob_t_done")
        pv_done, ohi_done, olo_done = s("pv_done"), s("ohi_done"), s("olo_done")
        HALF = [slice(0, 64), slice(64, 128)]
        heads = [("f", q_fox, k_fox, FOX_K, NOPE ** -0.5, 1, i) for i in range(HEADS)] + \
                [("k", q_mla, k_mla, QK, QK ** -0.5, 0, i) for i in range(HEADS)]
        NHD = len(heads)
        SPAN = [(0, P, 0), (P, 2 * P, P), (2 * P, T0, 3 * P)]

        block = ctx.enter_context(nc.Block())

        @block.sync
        def _(sp):
            sp.dma_start(params[:, :], params_in).then_inc(small_in, 16)

            def slabs(src, first, n, cols, rnd0):
                def body(i, wait=True):
                    for k in range(RAW):
                        if wait:
                            sp.wait_ge(wlo_done, i * UB + ((rnd0 - 1) * UB + 2 * k + 2))
                        sp.dma_start(raw[:, k, 0:cols], src[first + k + i * RAW]).then_inc(raw_full[k], 16)
                if rnd0 == 0:
                    body(0, wait=False)
                    sp.dma_start(q_fox[64:FOX_K, :, :], pad_in[0]).then_inc(pad_done, 16)
                    sp.dma_start(k_fox[64:FOX_K, :, :], pad_in[1]).then_inc(pad_done, 16)
                    with sp.Fori(1, n) as i:
                        body(i)
                else:
                    with sp.Fori(0, n) as i:
                        body(i)
            at = {8: 0, 6: 0}
            names = list(ph)
            g = 0
            while g < len(names):
                e = g
                while e < len(names) and ph[names[e]].blocks == ph[names[g]].blocks:
                    e += 1
                blocks = ph[names[g]].blocks
                n = sum(ph[x].bodies for x in names[g:e])
                slabs(w8 if blocks == 8 else w6, at[blocks], n, 2 * blocks * P, ph[names[g]].unit0 // UB)
                at[blocks] += n * RAW
                g = e
            for kt in range(KT):
                sp.wait_ge(out_ready, kt + 1)
                sp.dma_start(out[:, kt, :], h[:, kt, META:T0]).then_inc(out_done, 16)
            sp.wait_ge(out_done, 16 * KT)

        @block.tensor
        def _(pe):
            p = ph["attn_in"]
            pe.wait_ge(consts_in_done, 16)
            t = [0]

            def take():
                if t[0] >= 4:
                    pe.wait_ge(tile_free, t[0] - 3)
                t[0] += 1
                return (t[0] - 1) % 4

            def whole(u):
                bank = take()
                need = (lambda b: pe.wait_ge(xlo_done, b + 1)) if u == 0 else None
                mm = unit(pe, u // UB, u % UB, [(ps[:, bank, 0:T0], b == 0, b == 7) for b in range(8)],
                          [x_rhs(b, 0, T0) for b in range(8)], need)
                mm.then_inc(unit_done, 1)
                if u == 1:
                    pe_stats(pe, 0, 0, T0)

            def head_stats(n, which=range(HEADS)):
                rows = QKS[n][2]
                for hd in which:
                    pe.wait_ge(n_sq[n], hd + 1 if n == 3 else 1)
                    mm = nc.tensor.matmul(ps[0:HEADS, 6 + n % 2, 0:T0],
                                          consts[0:rows, K_SEL + HEADS * hd:K_SEL + HEADS * (hd + 1)],
                                          wide3[0:rows, hd, :], start=hd == 0, stop=hd == HEADS - 1)
                    if hd == HEADS - 1:
                        mm.then_inc(n_ss, 1)

            def head_spread(n):
                pe.wait_ge(n_inv, n + 1)
                for hd in range(HEADS):
                    k = n * HEADS + hd
                    if k >= 2:
                        pe.wait_ge(n_out, k - 1)
                    nc.tensor.matmul(ps[:, 4 + k % 2, 0:T0], sel_rows[:, hd, :], rms[:, n % 2, :], start=True,
                                     stop=True).then_inc(n_sp, 1)

            for u in range(0, U_FK):
                whole(u)
            pe.wait_ge(c_sq, 5)
            for i in range(5):
                mm = nc.tensor.matmul(ps[:, 4 + (i >= 3), 0:T0], ones, wide3[:, i, :], start=i in (0, 3),
                                      stop=i in (2, 4))
                if i in (2, 4):
                    mm.then_inc(c_ss, 1)
            for u in range(U_FK, U_FV):
                whole(u)
            head_stats(0)
            for u in range(U_FV, U_KN):
                whole(u)
            pe.wait_ge(c_root, 2)
            pe.wait_ge(rows_loaded, 16)
            head_spread(0)
            head_stats(1)

            pe.wait_ge(c_lo, 5)
            for u in (U_KN, U_V):
                pe.wait_ge(wlo_done, u + 1)
                for i in range(4):
                    bank = take()
                    o = ps[:, bank, 0:T0]
                    for kt in range(2):
                        b = 2 * i + kt
                        xh, xl = x_rhs(3 + kt, 0, T0, chi, clo)
                        hi, lo = whi[:, u % HLR, b * P:b * P + P], wlo[:, u % HLR, b * P:b * P + P]
                        nc.tensor.matmul(o, hi, xh, start=kt == 0, stop=False)
                        nc.tensor.matmul(o, hi, xl, start=False, stop=False)
                        mm = nc.tensor.matmul(o, lo, xh, start=False, stop=kt == 1)
                    if i == 3:
                        mm.then_inc(unit_done, 1)
                    else:
                        mm.then_inc(s("inner_tile"), 1)
            head_spread(1)
            for hd in range(HEADS):
                bank = take()
                o = ps[:, bank, 0:T0]
                for kt in range(3):
                    g = 3 * hd + kt
                    u, b = U_Q + g // 8, g % 8
                    if b == 0:
                        pe.wait_ge(wlo_done, u + 1)
                    if g == 3 * HEADS - 1:
                        pe.wait_ge(wlo_done, u + 2)
                    xh, xl = x_rhs(kt, 0, T0, chi, clo)
                    hi, lo = whi[:, u % HLR, b * P:b * P + P], wlo[:, u % HLR, b * P:b * P + P]
                    nc.tensor.matmul(o, hi, xh, start=kt == 0, stop=False)
                    nc.tensor.matmul(o, hi, xl, start=False, stop=False)
                    mm = nc.tensor.matmul(o, lo, xh, start=False, stop=kt == 2)
                    if b == 7:
                        mm.then_inc(unit_done, 2 if u == U_Q + 2 else 1)
                    elif kt == 2:
                        mm.then_inc(s("inner_tile"), 1)
                if hd == 0:
                    head_stats(2)
                if hd == 3:
                    head_spread(2)
                if hd == 4:
                    head_stats(3, range(0, 4))
                if hd >= 5:
                    head_stats(3, [hd - 1])
            pe.wait_ge(tile_free, TL_V + 4)
            pe.wait_ge(n_out, 3 * HEADS)
            for k in range(6):
                w, kt = k // 3, k % 3
                a, n = kt * P, min(P, T0 - kt * P)
                if k >= 2:
                    pe.wait_ge(vt_done, k - 1)
                for i in range(4):
                    mm = nc.tensor.transpose(ps[0:n, 4 + k % 2, i * P:(i + 1) * P], v_fm[:, w, i, a:a + n], ident)
                mm.then_inc(vt_ps, 1)
                if k == 2:
                    head_stats(3, [HEADS - 1])
            pe.wait_ge(vt_done, 6)
            head_spread(3)

            def scores(i):
                kind, q, k, rows, _, _, hd = heads[i]
                b = 4 * (i % 2)
                if i == 0:
                    pe.wait_ge(fox_done, 2)
                    pe.wait_ge(tile_free, N_TL)
                    pe.wait_ge(n_root, 4)
                if i == 1:
                    pe.wait_ge(n_out, 4 * HEADS)
                if kind == "k" and hd == 0:
                    pe.wait_ge(rope_done, 2)
                if i >= 2:
                    pe.wait_ge(ex_done, 3 * (i - 1))
                for r, (a, to, _) in enumerate(SPAN):
                    n = min(P, T0 - a)
                    o = ps[0:n, b, a:a + to] if r < 2 else ps[0:n, b + 1, 0:to]
                    nc.tensor.matmul(o, q[0:rows, hd, a:a + n], k[0:rows, hd, 0:to], start=True, stop=False)
                    mm = nc.tensor.matmul(o[:, a:to], ident[:, 0:n], mask[:, 0:n], start=False, stop=True)
                mm.then_inc(sc_done, 1)

            def turn(i):
                b = 4 * (i % 2) + 2
                pr = prob[i % 3]
                pe.wait_ge(pn_done, 3 * i + 3)
                if i >= 2:
                    pe.wait_ge(pt_done, 2 * (i - 1))
                at = 0
                for kt in range(3):
                    nk = min(P, T0 - kt * P)
                    for r in range(kt, 3):
                        a, to, col = SPAN[r]
                        n = min(P, T0 - a)
                        mm = nc.tensor.transpose(ps[0:nk, b, at:at + n], pr[0:n, col + kt * P:col + kt * P + nk],
                                                 ident[0:n, 0:n])
                        at += n
                mm.then_inc(pt_ps, 1)

            def values(i):
                _, _, _, _, _, w, hd = heads[i]
                b = 4 * (i % 2) + 3
                pt = prob_t[i % 2]
                pe.wait_ge(pt_done, 2 * i + 2)
                if i >= 2:
                    pe.wait_ge(olo_done, i - 1)
                r0 = 64 * (hd % 2)
                at = 0
                for kt in range(3):
                    nk = min(P, T0 - kt * P)
                    n = T0 - kt * P
                    mm = nc.tensor.matmul(ps[r0:r0 + DV, b, kt * P:T0], v_tok[0:nk, w, kt, hd * DV:(hd + 1) * DV],
                                          pt[0:nk, at:at + n], start=kt == 0, stop=kt == 2)
                    at += n
                mm.then_inc(pv_done, 1)

            for st in range(NHD + 3):
                if st < NHD:
                    scores(st)
                if 2 <= st < NHD + 2:
                    turn(st - 2)
                if st >= 3:
                    values(st - 3)

            pe_wide(pe, ph["attn_out"], C1, T1, 1, (chi, clo), (olo_done, 0, 2), after_attention=True)
            pe_wide(pe, ph["mlp0_up"], C1, T1, 1, (xhi, xlo), from_x(1), norm=1)
            pe_wide(pe, ph["mlp0_down"], 0, T1, 4, (hhi1, hlo1), from_hidden("mlp0_down"))
            pe_wide(pe, ph["conv_in"], C1, T1, 1, (xhi, xlo), from_x(2), norm=2)
            pe_wide(pe, ph["conv_out"], 0, SEQ, 1, (hhi1, hlo1), from_hidden("conv_out"))
            pe_wide(pe, ph["mlp1_up"], META, SEQ, 1, (xhi, xlo), from_x(3), norm=3)
            pe_wide(pe, ph["mlp1_down"], 0, SEQ, 4, (hhi1, hlo1), from_hidden("mlp1_down"))
            pe_wide(pe, ph["a_v"], META, SEQ, 1, (xhi, xlo), from_x(4), norm=4)
            pe.wait_ge(s("av_ssum"), NA + 1)
            for c in range(2):
                mm = nc.tensor.matmul(ps[:, 4, c:c + 1], ssum[:, META + c * P:META + (c + 1) * P], ones[:, 0:1],
                                      start=True, stop=True)
            mm.then_inc(s("av_stat"), 1)
            for g in range(NA // 2):
                c, f = g // 4, g % 4
                if g >= 2:
                    pe.wait_ge(s("av_tok"), g - 1)
                for i in range(4):
                    mm = nc.tensor.transpose(ps[:, 5 + g % 2, i * P:(i + 1) * P],
                                             v_a[:, 4 * f + i, c * P:(c + 1) * P], ident)
                mm.then_inc(s("av_turned"), 1)
            pe.wait_ge(s("av_tok"), 8)
            pe.wait_ge(s("ws_scaled"), 2)
            for f in range(NA):
                if f >= 2:
                    pe.wait_ge(s("sv_done"), f - 1)
                for c in range(2):
                    mm = nc.tensor.matmul(ps[:, 4 + 3 * (f % 2), c * P:(c + 1) * P],
                                          v_atok[:, c, f * P:(f + 1) * P], ws_s[:, c, (f // 2) * P:(f // 2 + 1) * P],
                                          start=True, stop=True)
                mm.then_inc(s("sv_ps"), 1)
            pe_wide(pe, ph["a_u"], META, SEQ, 1, (xhi, xlo), from_x(4))
            pe_wide(pe, ph["a_out"], 0, SEQ, 2, (hhi2, hlo2), from_hidden("a_out"))
            pe_stats(pe, 5, META, SEQ)
            pe_wide(pe, ph["f0_up"], META, SEQ, 1, (xhi, xlo), from_x(5))
            pe_wide(pe, ph["f0_down"], 0, SEQ, 4, (hhi2, hlo2), from_hidden("f0_down"))
            p = ph["b_in"]
            t[0] = 0

            def take_b():
                pe.wait_ge(tile_free, p.tile0 + t[0] - 3)
                t[0] += 1
                return (t[0] - 1) % 4

            def whole_b(k):
                bank = take_b()
                u = p.unit0 + k
                if k == 29:
                    pe.wait_ge(wlo_done, p.unit0 + 32)
                unit(pe, u // UB, u % UB, [(ps[:, bank, 0:SEQ], b == 0, b == 7) for b in range(8)],
                     [x_rhs(b, META, SEQ) for b in range(8)],
                     (lambda b: pe.wait_ge(xlo_done, 8 * 6 + b + 1)) if k == 0 else None)\
                    .then_inc(unit_done, 3 if k == 29 else 1)
            for k in range(NB):
                whole_b(k)
                if k == 1:
                    pe_stats(pe, 6, META, SEQ)
            pe.wait_ge(ulo_done, hid0["b_x"] + NB)
            for hd in range(NB // 2):
                u = p.unit0 + NB + hd
                pe.wait_ge(wlo_done, u + 1)
                for i in range(4):
                    bank = take_b()
                    o = ps[:, bank, 0:SEQ]
                    for kt in range(2):
                        b = 2 * i + kt
                        xh, xl = x_rhs(2 * hd + kt, 0, SEQ, hhi2, hlo2)
                        hi, lo = whi[:, u % HLR, b * P:b * P + P], wlo[:, u % HLR, b * P:b * P + P]
                        nc.tensor.matmul(o, hi, xh, start=kt == 0, stop=False)
                        nc.tensor.matmul(o, hi, xl, start=False, stop=False)
                        mm = nc.tensor.matmul(o, lo, xh, start=False, stop=kt == 1)
                    mm.then_inc(unit_done if i == 3 else s("inner_tile"), 1)
            for k in range(18, 30):
                whole_b(k)
            pe_wide(pe, ph["b_out"], 0, SEQ, 2, (hhi2, hlo2), from_hidden("b_out"))
            pe_stats(pe, 7, META, SEQ)
            pe_wide(pe, ph["f1_up"], META, SEQ, 1, (xhi, xlo), from_x(7))
            pe_wide(pe, ph["f1_down"], 0, SEQ, 4, (hhi2, hlo2), from_hidden("f1_down"))
            pe_stats(pe, 8, META, SEQ)

        @block.vector
        def _(dve):
            dve.wait_ge(small_in, 16)
            dve.wait_ge(x_loaded, 16)
            for kt in range(KT):
                dve_gain(dve, 0, kt, kt % 2, 0, T0)
                if kt == 2:
                    split_lo(dve, 0, 0, 8)
            for j in range(1, LA):
                split_lo(dve, 0, j, 8)
            nc.vector.memset(soft[:, :, :, :], 1.0).then_inc(s("soft_set"), 1)
            split_lo(dve, 0, LA, 8)
            dve_rstd(dve, 0, 0, T0)

            p = ph["attn_in"]
            done = [1]

            def to(u):
                while done[0] <= u:
                    j = done[0] % UB
                    ahead(dve, split_lo, p, done[0] // UB, j, done[0] // UB == p.bodies - 1)
                    done[0] += 1

            def inverse(n):
                dve.wait_ge(n_root, n + 1)
                nc.vector.reciprocal(rms[:, n % 2, :], rms[:, n % 2, :]).then_inc(n_inv, 1)

            def head_normed(n):
                _, x, rows, g = QKS[n]
                rr = P if rows == QK else rows
                for hd in range(HEADS):
                    k = n * HEADS + hd
                    dve.wait_ge(n_sp, k + 1)
                    nc.vector.scalar_tensor_tensor(out=x[0:rr, hd, :], in0=x[0:rr, hd, :],
                                                   scalar=par(g, rows=slice(0, rr)), in1=ps[0:rr, 4 + k % 2, 0:T0],
                                                   op0=ALU.mult, op1=ALU.mult).then_inc(n_out, 1)

            def rope_sum(n):
                x, a = QKS[n][1], slice(64, 96)
                dve.wait_ge(rope_cos, n - 1)
                dve.wait_ge(rope_sin, n - 1)
                nc.vector.tensor_tensor(x[a, :, :], x[a, :, :], turned[a, :, :], ALU.add).then_inc(rope_done, 1)

            for t in range(N_TL):
                u = tile_unit[t]
                to(u)
                if u < 18:
                    dve.wait_ge(unit_done, u + 1)
                else:
                    full = [x for x in range(18, t + 1) if x in (21, 25, 28, 31, 33)]
                    if t in (21, 25, 33):
                        dve.wait_ge(unit_done, u + 1)
                    else:
                        dve.wait_ge(s("inner_tile"), sum(1 for x in range(18, t + 1) if x not in (21, 25, 33)))
                src = ps[:, t % 4, 0:T0]
                if t == 0:
                    nc.vector.tensor_tensor(fg[0:8, 0, :], src[0:8, :], rstd[0:8, :], ALU.mult).then_inc(s("logit"), 1)
                    nc.vector.tensor_tensor(k_pe[64:128, :], src[64:128, :], rstd[64:128, :],
                                            ALU.mult).then_inc(tile_free, 1)
                elif t < TL_FQ:
                    i = t - TL_CQ
                    nc.vector.tensor_tensor(c_raw[:, i, :], src, rstd[:, :], ALU.mult).then_inc(tile_free, 1)
                    dve.wait_ge(tile_free, t + 1)
                    g = par("g_cq", i) if i < 3 else par("g_ckv", i - 3)
                    if i >= 2:
                        dve.wait_ge(c_lo, i - 1)
                    nc.vector.tensor_scalar(tmp[:, i % 2, :], c_raw[:, i, :], g, None, ALU.mult).then_inc(c_g, 1)
                elif t < TL_FV or TL_KN <= t < TL_V:
                    x, i = (q_fox, t - TL_FQ) if t < TL_FK else (k_fox, t - TL_FK) if t < TL_FV else (k_mla, t - TL_KN)
                    r = rs_c[:, 1, :] if x is k_mla else rstd[:, :]
                    for o in range(2):
                        ins = nc.vector.tensor_tensor(x[0:64, 2 * i + o, :], src[HALF[o], :], r[HALF[o], :], ALU.mult)
                        ins.then_inc(tile_free if o else s("half_tile"), 1)
                elif t < TL_KN:
                    nc.vector.tensor_tensor(v_fm[:, 1, t - TL_FV, :], src, rstd[:, :], ALU.mult).then_inc(tile_free, 1)
                elif t < TL_Q:
                    nc.vector.tensor_tensor(v_fm[:, 0, t - TL_V, :], src, rs_c[:, 1, :], ALU.mult).then_inc(tile_free, 1)
                else:
                    nc.vector.tensor_tensor(q_mla[:, t - TL_Q, :], src, rs_c[:, 0, :], ALU.mult).then_inc(tile_free, 1)
                if t == TL_FK:
                    for i in range(2):
                        dve.wait_ge(c_root, i + 1)
                        nc.vector.reciprocal(rs_c[:, i, :], rs_c[:, i, :]).then_inc(c_rstd, 1)
                    dve.wait_ge(c_rstd, 2)
                if t == TL_FK + 2:
                    dve.wait_ge(s("logit"), 1)
                    nc.vector.tensor_scalar(fg[0:8, 0, :], fg[0:8, 0, :], par("b_forget", rows=slice(0, 8)), None,
                                            ALU.add).then_inc(s("logit"), 1)
                    dve.wait_ge(s("logit"), 2)
                    dve_log_sigmoid(dve, fg[0:8, 0, :], fg[0:8, 1, :], fg[0:8, 2, :], fg[0:8, 3, :], fg[0:8, 4, :],
                                    s("fg_step"), s("fg_exp_asked"), s("fg_exp"))
                    nc.vector.tensor_tensor_scan(fg[0:8, 1, :], ones[0:8, 0:1].broadcast_to([8, T0]), fg[0:8, 4, :],
                                                 0.0, ALU.mult, ALU.add).then_inc(s("fg_sum"), 1)
                if t == TL_FV + 1:
                    inverse(0)
                if t == TL_KN - 1:
                    head_normed(0)
                if t == TL_KN + 1:
                    inverse(1)
                if t == TL_Q - 1:
                    head_normed(1)
                if t == TL_Q + 2:
                    inverse(2)
                if t == TL_Q + 3:
                    head_normed(2)
            to(p.units - 1)
            inverse(3)
            head_normed(3)
            dve.wait_ge(s("soft_set"), 1)

            def peak(i):
                b, sf = 4 * (i % 2), soft[:, i % 2, :, :]
                dve.wait_ge(sc_done, i + 1)
                if i >= 2:
                    dve.wait_ge(pn_done, 3 * (i - 1))
                for r, (a, to_, _) in enumerate(SPAN):
                    n = min(P, T0 - a)
                    src = ps[0:n, b, a:a + to_] if r < 2 else ps[0:n, b + 1, 0:to_]
                    nc.vector.tensor_reduce(sf[0:n, 0, r:r + 1], src, AX.X, ALU.max).then_inc(mx_done, 1)
                dve.wait_ge(mx_done, 3 * i + 3)
                nc.vector.tensor_scalar(sf[:, 1, :], sf[:, 0, :], -heads[i][4], None, ALU.mult).then_inc(nb_done, 1)

            def normal(i):
                sf = soft[:, i % 2, :, :]
                dve.wait_ge(ex_done, 3 * i + 3)
                nc.vector.reciprocal(sf[:, 3, :], sf[:, 2, :]).then_inc(rc_done, 1)
                dve.wait_ge(rc_done, i + 1)
                for r, (a, to_, col) in enumerate(SPAN):
                    n = min(P, T0 - a)
                    pr = prob[i % 3][0:n, col:col + to_]
                    nc.vector.tensor_scalar(pr, pr, sf[0:n, 3, r:r + 1], None, ALU.mult).then_inc(pn_done, 1)

            def low(i):
                w, hd = heads[i][5:7]
                rows = HALF[hd % 2]
                dve.wait_ge(ohi_done, i + 1)
                nc.vector.tensor_tensor(clo[rows, 4 * (1 - w) + hd // 2, :], ps[rows, 4 * (i % 2) + 3, 0:T0],
                                        chi[rows, 4 * (1 - w) + hd // 2, :].bitcast(F32), ALU.subtract).then_inc(olo_done, 1)
            for st in range(NHD + 3):
                if 1 <= st <= NHD:
                    normal(st - 1)
                if st < NHD:
                    peak(st)
                if st >= 3:
                    low(st - 3)
                if st in (2, 6):
                    rope_sum(2 if st == 2 else 3)
            dve_log_sigmoid(dve, par("lam", 0, NB), log_lam[:, :], tmp[:, 0, 0:NB], tmp[:, 1, 0:NB],
                            tmp[:, 0, NB:2 * NB], s("lam_step"), s("lam_exp_asked"), s("lam_exp"))
            nc.vector.tensor_scalar(log_lam[:, :], tmp[:, 0, NB:2 * NB], 8.0, None, ALU.mult).then_inc(s("lam_done"), 1)

            dve_residual(dve, ph["attn_out"], 1, 1, C1, T1)
            dve_rstd(dve, 1, C1, T1, ph["mlp0_up"])
            dve_mlp_up(dve, ph["mlp0_up"], C1, T1)
            dve_residual(dve, ph["mlp0_down"], 4, 2, C1, T1)
            dve_rstd(dve, 2, C1, T1, ph["conv_in"])
            p = ph["conv_in"]
            for it in range(3):
                for j in range(UB):
                    ahead(dve, split_lo, p, it, j, it == 2)
                    k = it * UB + j
                    dve.wait_ge(unit_done, p.unit0 + k + 1)
                    src = ps[:, j % 4, 0:T1]
                    if it == 0:
                        nc.vector.tensor_tensor(gate_c[:, j, :], src, rstd[:, C1:T0], ALU.mult).then_inc(tile_free, 1)
                        continue
                    x = tmp[:, j % 2, 0:T1]
                    nc.vector.tensor_tensor(x, src, rstd[:, C1:T0], ALU.mult).then_inc(tile_free, 1)
                    dve.wait_ge(tile_free, p.tile0 + k + 1)
                    if it == 1:
                        g, y, c = gate_c[:, j, :], conv_y[:, j, :], s("conv_step")
                        nc.vector.tensor_tensor(g, x, g, ALU.mult).then_inc(c, 1)
                        dve.wait_ge(c, 4 * j + 1)
                        nc.vector.tensor_scalar(y, g[:, 0:SEQ], par("conv_w", 3 * j), None, ALU.mult).then_inc(c, 1)
                        for tap in (1, 2):
                            dve.wait_ge(c, 4 * j + 1 + tap)
                            nc.vector.scalar_tensor_tensor(out=y, in0=g[:, tap:tap + SEQ],
                                                           scalar=par("conv_w", 3 * j + tap), in1=y,
                                                           op0=ALU.mult, op1=ALU.add).then_inc(c, 1)
                    else:
                        dve.wait_ge(s("conv_step"), 32)
                        dve.wait_ge(ulo_done, hid0["conv_in"] + j - 1)
                        nc.vector.tensor_tensor(act1[:, j % 2, 0:SEQ], x[:, HALO:T1], conv_y[:, j, :],
                                                ALU.mult).then_inc(u_done, 1)
            dve_residual(dve, ph["conv_out"], 1, 3, META, SEQ)
            dve_rstd(dve, 3, META, SEQ, ph["mlp1_up"])
            dve_mlp_up(dve, ph["mlp1_up"], META, SEQ)
            dve_residual(dve, ph["mlp1_down"], 4, 4, META, SEQ)
            dve_rstd(dve, 4, META, SEQ, ph["a_v"])

            def scaled(p, ready):
                def body(it, last):
                    for j in range(UB):
                        k = it * UB + j
                        dve.wait_ge(unit_done, k + (p.unit0 + 1))
                        if not isinstance(k, int) or k >= 2:
                            dve.wait_ge(ready, k - 1)
                        nc.vector.tensor_tensor(tmp[:, j % 2, 0:SEQ], ps[:, j % 4, 0:SEQ], rstd[:, META:T0],
                                                ALU.mult).then_inc(tile_free, 1)
                        ahead(dve, split_lo, p, it, j, last)
                loop_peeled(dve, p.bodies, body)
            scaled(ph["a_v"], s("av_gelu"))
            dve.wait_ge(s("av_root"), 1)
            nc.vector.reciprocal(root[:, 2:4], root[:, 0:2]).then_inc(s("av_rstd"), 1)
            dve.wait_ge(s("av_rstd"), 1)
            dve.wait_ge(s("ws_masked"), 1)
            for c in range(2):
                nc.vector.tensor_scalar(ws_s[:, c, :], ws[:, :], root[:, 2 + c:3 + c], None,
                                        ALU.mult).then_inc(s("ws_scaled"), 1)
            dve.wait_ge(s("bs_loaded"), 16)
            dve.wait_ge(s("av_tok"), 8)
            for f in range(NA):
                dve.wait_ge(s("sv_ps"), f + 1)
                b3 = bs[:, f // 2, :].unsqueeze(1).broadcast_to([P, 2, P])
                nc.vector.scalar_tensor_tensor(
                    out=v_a[:, f, :].rearrange("p (c n) -> p c n", c=2),
                    in0=ps[:, 4 + 3 * (f % 2), 0:SEQ].rearrange("p (c n) -> p c n", c=2),
                    scalar=par("v_gain", f), in1=b3, op0=ALU.mult, op1=ALU.add).then_inc(s("sv_done"), 1)
            scaled(ph["a_u"], s("au_gelu"))
            dve_residual(dve, ph["a_out"], 2, 5, META, SEQ)
            dve_rstd(dve, 5, META, SEQ)
            dve_pre(dve, 5, META, SEQ)
            dve_ffn_up(dve, ph["f0_up"], 0)
            dve_residual(dve, ph["f0_down"], 4, 6, META, SEQ)
            dve_rstd(dve, 6, META, SEQ, ph["b_in"])

            p = ph["b_in"]
            dve.wait_ge(s("lam_done"), 1)
            for k in range(NB):
                ahead(dve, split_lo, p, k // UB, k % UB, False)
                dve.wait_ge(unit_done, p.unit0 + k + 1)
                x, y = tmp[:, k % 2, 0:SEQ], xb[:, k, :]
                nc.vector.tensor_tensor(x, ps[:, k % 4, 0:SEQ], rstd[:, META:T0], ALU.mult).then_inc(tile_free, 1)
                dve.wait_ge(tile_free, p.tile0 + k + 1)
                c = s("b_conv_step")
                nc.vector.tensor_scalar(y, x, par("b_conv_w", 4 * k + 3), par("b_conv_b", k), ALU.mult,
                                        ALU.add).then_inc(c, 1)
                for tap in (2, 1, 0):
                    o = 3 - tap
                    dve.wait_ge(c, 3 * k + o)
                    ins = nc.vector.scalar_tensor_tensor(out=y[:, o:SEQ], in0=x[:, 0:SEQ - o],
                                                         scalar=par("b_conv_w", 4 * k + tap), in1=y[:, o:SEQ],
                                                         op0=ALU.mult, op1=ALU.add)
                    ins.then_inc(c if tap else u_done, 1)
            for k in range(NB, NB + 6):
                ahead(dve, split_lo, p, k // UB, k % UB, False)
            for k in range(18, 32):
                ahead(dve, split_lo, p, k // UB, k % UB, k // UB == 3)
                if k >= 30:
                    continue
                t = k - 18
                dve.wait_ge(unit_done, p.unit0 + k + (3 if k == 29 else 1))
                nc.vector.tensor_tensor(h_gate(t), ps[:, t % 4, 0:SEQ], rstd[:, META:T0], ALU.mult).then_inc(tile_free, 1)
                dve.wait_ge(s("b_tanh"), t + 1)
                a, th, sq_ = decay[:, t, :], work1[:, t, :], tmp[:, t % 2, 0:SEQ]
                nc.vector.tensor_tensor(sq_, a, a, ALU.mult).then_inc(s("b_aa"), 1)
                dve.wait_ge(s("b_aa"), t + 1)
                nc.vector.scalar_tensor_tensor(out=th, in0=sq_, scalar=1.0, in1=th, op0=ALU.add,
                                               op1=ALU.mult).then_inc(s("b_m2"), 1)
            for t in range(NB):
                bt, a, hs = xb[:, t, :], decay[:, t, :], work1[:, t, :]
                dve.wait_ge(s("b_term"), t + 1)
                nc.vector.tensor_tensor_scan(hs, a, bt, 0.0, ALU.mult, ALU.add).then_inc(s("b_scan"), 1)
            for t in range(NB):
                dve.wait_ge(s("b_scan"), NB)
                dve.wait_ge(s("b_gelu"), t + 1)
                nc.vector.tensor_tensor(xb[:, t, :], work1[:, t, :], h_gate(t), ALU.mult).then_inc(u_done, 1)
            dve_residual(dve, ph["b_out"], 2, 7, META, SEQ)
            dve_rstd(dve, 7, META, SEQ)
            dve_pre(dve, 7, META, SEQ)
            dve_ffn_up(dve, ph["f1_up"], 1)
            dve_residual(dve, ph["f1_down"], 4, 8, META, SEQ)
            dve_rstd(dve, 8, META, SEQ)
            for kt in range(KT):
                hh = h[:, kt, META:T0]
                nc.vector.scalar_tensor_tensor(out=hh, in0=hh, scalar=par("norm_final", kt), in1=rstd[:, META:T0],
                                               op0=ALU.mult, op1=ALU.mult).then_inc(out_ready, 1)

        @block.scalar
        def _(act):
            act.dma_start(h[:, :, :], x_in).then_inc(x_loaded, 16)
            act.dma_start(consts[:, :], consts_in).then_inc(consts_in_done, 16)
            act.dma_start(sel_rows[:, :, :], rows_in).then_inc(rows_loaded, 16)
            split_hi(act, 0, 0, 8, first=True)
            for kt in range(KT):
                act_xhi(act, 0, kt, kt % 2, 0, T0)
                if kt in (3, 6):
                    split_hi(act, 0, kt // 3, 8, first=True)
            for kt in range(KT):
                act_square(act, 0, kt, kt % 2, 0, T0)
            split_hi(act, 0, LA, 8, first=True)
            act_root(act, 0, 0, T0)

            p = ph["attn_in"]
            done = [1]

            def to(u):
                while done[0] <= u:
                    j = done[0] % UB
                    rnd = done[0] // UB + (j + LA) // UB
                    split_hi(act, rnd, (j + LA) % UB, 8, first=rnd == 0)
                    done[0] += 1

            def roots(n):
                act.wait_ge(n_ss, n + 1)
                if n >= 2:
                    act.wait_ge(n_sp, (n - 1) * HEADS)
                nc.scalar.activation(rms[:, n % 2, :], ps[0:HEADS, 6 + n % 2, 0:T0], ACT.Sqrt,
                                     scale=1.0 / QKS[n][2], bias=par("eps", rows=slice(0, HEADS))).then_inc(n_root, 1)

            def squares(n):
                _, x, rows, _ = QKS[n]
                if n:
                    act.wait_ge(n_ss, n)
                else:
                    act.wait_ge(c_ss, 2)
                act.wait_ge(tile_free, [TL_FQ + 4, TL_FK + 4, TL_KN + 4][n])
                if n == 2:
                    act.wait_ge(kpe_done, 1)
                nc.scalar.activation(wide3[0:rows, :, :], x[0:rows, :, :], ACT.Square).then_inc(n_sq[n], 1)

            for t in range(N_TL):
                to(tile_unit[t])
                if TL_CQ <= t < TL_FQ:
                    i = t - TL_CQ
                    act.wait_ge(c_g, i + 1)
                    nc.scalar.activation(chi[:, i, :], tmp[:, i % 2, :], ACT.Copy).then_inc(c_hi, 1)
                    nc.scalar.activation(wide3[:, i, :], c_raw[:, i, :], ACT.Square).then_inc(c_sq, 1)
                if t == TL_FK:
                    for i in range(2):
                        act.wait_ge(c_ss, i + 1)
                        nc.scalar.activation(rs_c[:, i, :], ps[:, 4 + i, 0:T0], ACT.Sqrt,
                                             scale=1.0 / (384, 256)[i], bias=par("eps")).then_inc(c_root, 1)
                    squares(0)
                if t == TL_FK + 2:
                    act.wait_ge(s("fg_exp_asked"), 1)
                    nc.scalar.activation(fg[0:8, 1, :], fg[0:8, 1, :], ACT.Exp).then_inc(s("fg_exp"), 1)
                if t == TL_FV + 1:
                    roots(0)
                    squares(1)
                if t == TL_FV + 2:
                    act.wait_ge(s("fg_sum"), 1)
                    act.wait_ge(pad_done, 32)
                    f = fg[0:8, 1, :].unsqueeze(1).broadcast_to([8, HEADS, T0])
                    nc.scalar.activation(q_fox[64:72, :, :], f, ACT.Copy, scale=8.0).then_inc(fox_done, 1)
                    nc.scalar.activation(k_fox[96:104, :, :], f, ACT.Copy).then_inc(fox_done, 1)
                if t == TL_KN + 1:
                    roots(1)
                if t == TL_V + 1:
                    squares(2)
                if t == TL_Q + 2:
                    roots(2)
                if t >= TL_Q:
                    hd = t - TL_Q
                    if hd >= 3:
                        for x in (range(0, 4) if hd == 3 else [hd]):
                            act.wait_ge(n_ss, 3)
                            act.wait_ge(tile_free, TL_Q + x + 1)
                            nc.scalar.activation(wide3[0:QK, x, :], q_mla[0:QK, x, :],
                                                 ACT.Square).then_inc(n_sq[3], 1)
            to(p.units - 1)
            for k in range(6):
                w, kt = k // 3, k % 3
                n = min(P, T0 - kt * P)
                act.wait_ge(vt_ps, k + 1)
                nc.scalar.activation(v_tok[0:n, w, kt, :], ps[0:n, 4 + k % 2, :], ACT.Copy).then_inc(vt_done, 1)
                if k == 3:
                    roots(3)

            def exps(i):
                b, sf = 4 * (i % 2), soft[:, i % 2, :, :]
                act.wait_ge(nb_done, i + 1)
                if i >= 3:
                    act.wait_ge(pt_ps, i - 2)
                elif i < 2:
                    act.wait_ge(n_ss, 4)
                for r, (a, to_, col) in enumerate(SPAN):
                    n = min(P, T0 - a)
                    src = ps[0:n, b, a:a + to_] if r < 2 else ps[0:n, b + 1, 0:to_]
                    nc.scalar.activation(prob[i % 3][0:n, col:col + to_], src, ACT.Exp, bias=sf[0:n, 1, r:r + 1],
                                         scale=heads[i][4], accum_out=sf[0:n, 2, r:r + 1]).then_inc(ex_done, 1)

            def turned(i):
                b = 4 * (i % 2) + 2
                act.wait_ge(pt_ps, i + 1)
                if i >= 2:
                    act.wait_ge(pv_done, i - 1)
                nc.scalar.activation(prob_t[i % 2][:, 0:416], ps[:, b, 0:416], ACT.Copy).then_inc(pt_done, 1)
                nc.scalar.activation(prob_t[i % 2][0:META, 416:432], ps[0:META, b, 416:432],
                                     ACT.Copy).then_inc(pt_done, 1)

            def high(i):
                w, hd = heads[i][5:7]
                rows = HALF[hd % 2]
                act.wait_ge(pv_done, i + 1)
                nc.scalar.activation(chi[rows, 4 * (1 - w) + hd // 2, :], ps[rows, 4 * (i % 2) + 3, 0:T0],
                                     ACT.Copy).then_inc(ohi_done, 1)
            for st in range(NHD + 3):
                if st < NHD:
                    exps(st)
                if 2 <= st < NHD + 2:
                    turned(st - 2)
                if st >= 3:
                    high(st - 3)
            act.wait_ge(s("lam_exp_asked"), 1)
            nc.scalar.activation(log_lam[:, :], log_lam[:, :], ACT.Exp).then_inc(s("lam_exp"), 1)

            act_residual(act, ph["attn_out"], 1, 1, C1, T1)
            act_root(act, 1, C1, T1, ph["mlp0_up"])
            act_hidden(act, ph["mlp0_up"], hhi1, act1, T1)
            act_residual(act, ph["mlp0_down"], 4, 2, C1, T1)
            act_root(act, 2, C1, T1, ph["conv_in"])
            p = ph["conv_in"]
            for it in range(3):
                for j in range(UB):
                    ahead(act, split_hi, p, it, j, it == 2)
                    if it == 2:
                        act.wait_ge(u_done, hid0["conv_in"] + j + 1)
                        nc.scalar.activation(hhi1[:, j, 0:SEQ], act1[:, j % 2, 0:SEQ], ACT.Copy).then_inc(uhi_done, 1)
            act_residual(act, ph["conv_out"], 1, 3, META, SEQ)
            act_root(act, 3, META, SEQ, ph["mlp1_up"])
            act_hidden(act, ph["mlp1_up"], hhi1, act1, SEQ)
            act_residual(act, ph["mlp1_down"], 4, 4, META, SEQ)
            act_root(act, 4, META, SEQ, ph["a_v"])

            act.wait_ge(unit_done, ph["a_v"].unit0)
            act.dma_start(ws[:, :], ws_in).then_inc(s("ws_loaded"), 16)
            act.dma_start(bs[:, :, :], bs_in).then_inc(s("bs_loaded"), 16)
            p = ph["a_v"]

            def body(it, last):
                for j in range(UB):
                    ahead(act, split_hi, p, it, j, last)
                    k = it * UB + j
                    act.wait_ge(tile_free, k + (p.tile0 + 1))
                    nc.scalar.activation(v_a[:, k, :], tmp[:, j % 2, 0:SEQ], ACT.Gelu_apprx_tanh).then_inc(s("av_gelu"), 1)
            loop_peeled(act, p.bodies, body)
            act.wait_ge(s("av_stat"), 1)
            nc.scalar.activation(root[:, 0:2], ps[:, 4, 0:2], ACT.Sqrt, scale=1.0 / (2 * D),
                                 bias=par("eps")).then_inc(s("av_root"), 1)
            for g in range(NA // 2):
                c, f = g // 4, g % 4
                act.wait_ge(s("av_turned"), g + 1)
                nc.scalar.activation(v_atok[:, c, f * 512:(f + 1) * 512], ps[:, 5 + g % 2, :],
                                     ACT.Copy).then_inc(s("av_tok"), 1)
            p2 = ph["a_u"]

            def body_u(it, last):
                for j in range(UB):
                    ahead(act, split_hi, p2, it, j, last)
                    k = it * UB + j
                    act.wait_ge(tile_free, k + (p2.tile0 + 1))
                    act.wait_ge(u_done, k + (hid0["a_u"] - 1))
                    nc.scalar.activation(act2[:, j % 2, :], tmp[:, j % 2, 0:SEQ],
                                         ACT.Gelu_apprx_tanh).then_inc(s("au_gelu"), 1)
                    if k:
                        high_u(k - 1)

            def high_u(k):
                act.wait_ge(u_done, k + (hid0["a_u"] + 1))
                nc.scalar.activation(hhi2[:, k, :], xg[:, k % 2, 0:SEQ], ACT.Copy).then_inc(uhi_done, 1)
            loop_ends(act, p2.bodies, body_u)
            high_u(NA - 1)
            act_residual(act, ph["a_out"], 2, 5, META, SEQ)
            act_root(act, 5, META, SEQ)
            act_pre(act, 5, META, SEQ)
            act_ffn_up(act, ph["f0_up"], 0)
            act_residual(act, ph["f0_down"], 4, 6, META, SEQ)
            act_root(act, 6, META, SEQ, ph["b_in"])

            p = ph["b_in"]
            for k in range(NB):
                ahead(act, split_hi, p, k // UB, k % UB, False)
                act.wait_ge(u_done, hid0["b_x"] + k + 1)
                nc.scalar.activation(hhi2[:, k, :], xb[:, k, :], ACT.Copy).then_inc(uhi_done, 1)
            for hd in range(NB // 2):
                k = NB + hd
                ahead(act, split_hi, p, k // UB, k % UB, False)
                for i in range(4):
                    t = NB + 4 * hd + i
                    if i == 3:
                        act.wait_ge(unit_done, p.unit0 + k + 1)
                    else:
                        act.wait_ge(s("inner_tile"), 3 + 3 + 7 + (3 * hd + i + 1))
                    f = 2 * hd + i % 2
                    if i < 2:
                        nc.scalar.activation(work1[:, f, :], ps[:, t % 4, 0:SEQ], ACT.Sigmoid,
                                             bias=par("b_b_a", f)).then_inc(tile_free, 1)
                    else:
                        if f >= 2:
                            act.wait_ge(s("b_ix"), f - 1)
                        nc.scalar.activation(act2[:, f % 2, :], ps[:, t % 4, 0:SEQ], ACT.Sigmoid,
                                             bias=par("b_b_x", f)).then_inc(tile_free, 1)
            act.wait_ge(tile_free, p.tile0 + 3 * NB)
            act.wait_ge(s("lam_done"), 1)
            for k in range(18, 32):
                ahead(act, split_hi, p, k // UB, k % UB, k // UB == 3)
                t = k - 18
                if k < 30:
                    L = log_lam[:, t:t + 1]
                    nc.scalar.activation(decay[:, t, :], work1[:, t, :], ACT.Exp, scale=L).then_inc(s("b_exp"), 1)
                    act.wait_ge(s("b_exp"), t + 1)
                    nc.scalar.activation(work1[:, t, :], work1[:, t, :], ACT.Tanh, scale=L).then_inc(s("b_tanh"), 1)
            for t in range(NB):
                act.wait_ge(s("b_m2"), t + 1)
                nc.scalar.activation(work1[:, t, :], work1[:, t, :], ACT.Sqrt, scale=-1.0).then_inc(s("b_mult"), 1)
            for t in range(NB):
                act.wait_ge(tile_free, p.tile0 + 3 * NB + t + 1)
                nc.scalar.activation(h_gate(t), h_gate(t), ACT.Gelu_apprx_tanh).then_inc(s("b_gelu"), 1)
            for t in range(NB):
                act.wait_ge(u_done, hid0["b_in"] + t + 1)
                nc.scalar.activation(hhi2[:, t, :], xb[:, t, :], ACT.Copy).then_inc(uhi_done, 1)
            act_residual(act, ph["b_out"], 2, 7, META, SEQ)
            act_root(act, 7, META, SEQ)
            act_pre(act, 7, META, SEQ)
            act_ffn_up(act, ph["f1_up"], 1)
            act_residual(act, ph["f1_down"], 4, 8, META, SEQ)
            act_root(act, 8, META, SEQ)

        @block.gpsimd
        def _(pool):
            pool_clear(pool, 0)
            for kt in range(KT):
                pool_xlo(pool, 0, kt, kt % 2, 0, T0)
            for kt in range(KT):
                pool_ssum(pool, 0, kt, kt % 2, 0, T0)
            for i in range(5):
                pool.wait_ge(c_hi, i + 1)
                nc.gpsimd.tensor_tensor(clo[:, i, :], tmp[:, i % 2, :], chi[:, i, :].bitcast(F32),
                                        ALU.subtract).then_inc(c_lo, 1)
            pool.wait_ge(tile_free, 1)
            pool.wait_ge(c_lo, 5)
            src = k_pe[64:128, :].unsqueeze(1).broadcast_to([64, HEADS, T0])
            nc.gpsimd.tensor_copy(k_mla[64:128, :, :], src).then_inc(kpe_done, 1)
            pool.wait_ge(kpe_done, 1)
            pool.wait_ge(c_sq, 5)
            a, b = slice(64, 96), slice(96, 128)
            cos = consts[a, K_ROPE:K_ROPE + T0].unsqueeze(1).broadcast_to([32, HEADS, T0])
            sin = consts[b, K_ROPE:K_ROPE + T0].unsqueeze(1).broadcast_to([32, HEADS, T0])
            for n in (2, 3):
                x = QKS[n][1]
                pool.wait_ge(n_out, (n + 1) * HEADS)
                if n == 3:
                    pool.wait_ge(rope_done, 1)
                nc.gpsimd.tensor_tensor(turned[a, :, :], x[b, :, :], sin, ALU.mult).then_inc(rope_sin, 1)
                pool.wait_ge(rope_sin, n - 1)
                nc.gpsimd.tensor_tensor(x[a, :, :], x[a, :, :], cos, ALU.mult).then_inc(rope_cos, 1)
                pool.wait_ge(rope_cos, n - 1)
            pool_residual(pool, ph["attn_out"], 1, 1, C1, T1)
            pool_hidden(pool, ph["mlp0_up"], hhi1, hlo1, act1, T1)
            pool_residual(pool, ph["mlp0_down"], 4, 2, C1, T1)
            for j in range(UB):
                pool.wait_ge(uhi_done, hid0["conv_in"] + j + 1)
                nc.gpsimd.tensor_tensor(hlo1[:, j, 0:SEQ], act1[:, j % 2, 0:SEQ], hhi1[:, j, 0:SEQ].bitcast(F32),
                                        ALU.subtract).then_inc(ulo_done, 1)
            pool_residual(pool, ph["conv_out"], 1, 3, META, SEQ)
            pool_hidden(pool, ph["mlp1_up"], hhi1, hlo1, act1, SEQ)
            pool_residual(pool, ph["mlp1_down"], 4, 4, META, SEQ)
            c = s("av_ssum")
            pool.wait_ge(stat_done, 5)
            nc.gpsimd.memset(ssum[:, :], 0.0).then_inc(c, 1)

            def body(it):
                for j in range(UB):
                    k = it * UB + j
                    pool.wait_ge(s("av_gelu"), k + 1)
                    nc.gpsimd.tensor_tensor(sq[:, j % 2, 0:SEQ], v_a[:, k, :], v_a[:, k, :],
                                            ALU.mult).then_inc(s("av_square"), 1)
                    pool.wait_ge(s("av_square"), k + 1)
                    pool.wait_ge(c, k + 1)
                    nc.gpsimd.tensor_tensor(ssum[:, META:T0], ssum[:, META:T0], sq[:, j % 2, 0:SEQ],
                                            ALU.add).then_inc(c, 1)
            loop(pool, 2, body)
            pool.wait_ge(s("ws_loaded"), 16)
            w3 = ws[:, :].rearrange("p (g t) -> p g t", g=GROUPS)
            nc.gpsimd.affine_select(out=w3, in_=w3, compare_op=ALU.is_ge, fill=0.0, base=0,
                                    pattern=[[0, GROUPS], [1, P]], channel_multiplier=-1).then_inc(s("ws_masked"), 1)
            pool.wait_ge(s("sv_done"), NA)

            def low_u(k):
                pool.wait_ge(uhi_done, k + (hid0["a_u"] + 1))
                nc.gpsimd.tensor_tensor(hlo2[:, k, :], xg[:, k % 2, 0:SEQ], hhi2[:, k, :].bitcast(F32),
                                        ALU.subtract).then_inc(ulo_done, 1)
            for k in range(NA):
                pool.wait_ge(s("au_gelu"), k + 1)
                pool.wait_ge(ulo_done, hid0["a_u"] + k - 1)
                nc.gpsimd.tensor_tensor(xg[:, k % 2, 0:SEQ], act2[:, k % 2, :], v_a[:, k, :],
                                        ALU.mult).then_inc(u_done, 1)
                if k:
                    low_u(k - 1)
            low_u(NA - 1)
            pool.wait_ge(s("av_stat"), 1)
            pool_residual(pool, ph["a_out"], 2, 5, META, SEQ)
            pool_pre(pool, 5, META, SEQ)
            pool_ffn_up(pool, ph["f0_up"], 0)
            pool_residual(pool, ph["f0_down"], 4, 6, META, SEQ)
            for t in range(NB):
                pool.wait_ge(uhi_done, hid0["b_x"] + t + 1)
                nc.gpsimd.tensor_tensor(hlo2[:, t, :], xb[:, t, :], hhi2[:, t, :].bitcast(F32),
                                        ALU.subtract).then_inc(ulo_done, 1)
            tb = ph["b_in"].tile0 + NB
            for t in range(NB):
                pool.wait_ge(tile_free, tb + 4 * (t // 2) + 2 + t % 2 + 1)
                nc.gpsimd.tensor_tensor(xb[:, t, :], xb[:, t, :], act2[:, t % 2, :], ALU.mult).then_inc(s("b_ix"), 1)
            for t in range(NB):
                pool.wait_ge(s("b_mult"), t + 1)
                pool.wait_ge(s("b_ix"), t + 1)
                nc.gpsimd.tensor_tensor(xb[:, t, :], xb[:, t, :], work1[:, t, :], ALU.mult).then_inc(s("b_term"), 1)
            for t in range(NB):
                pool.wait_ge(uhi_done, hid0["b_in"] + t + 1)
                nc.gpsimd.tensor_tensor(hlo2[:, t, :], xb[:, t, :], hhi2[:, t, :].bitcast(F32),
                                        ALU.subtract).then_inc(ulo_done, 1)
            pool_residual(pool, ph["b_out"], 2, 7, META, SEQ)
            pool_pre(pool, 7, META, SEQ)
            pool_ffn_up(pool, ph["f1_up"], 1)
            pool_residual(pool, ph["f1_down"], 4, 8, META, SEQ)


def blocks_of(w):
    k, n = w.shape
    return w.reshape(k // P, P, n // P, P).transpose(0, 2, 1, 3)


def units_by_tile(w, blocks):
    b = blocks_of(w)
    kt, nt = b.shape[:2]
    return b.transpose(1, 0, 2, 3).reshape(nt * kt // blocks, blocks, P, P)


def slabs_of(units):
    u, b = units.shape[:2]
    return units.reshape(u // 2, 2, b, P, P).transpose(0, 3, 1, 2, 4).reshape(u // 2, P, 2 * b * P)


def pad_rows(a):
    return np.concatenate([a, np.zeros((P - a.shape[0],) + a.shape[1:], a.dtype)], 0)


def swapped(w):
    half = ROPE // 2
    nope, r = w[..., :NOPE], w[..., NOPE:]
    return np.concatenate([nope, r, r[..., half:], r[..., :half]], -1)


def lay_out(i):
    z = np.zeros
    f = np.float32
    w_in = i["w_in_attn"][0]
    c_q, c_kv, k_pe, fq, fk, fv, fl = np.split(w_in, np.cumsum([384, 256, 32, 512, 512, 512]), axis=1)
    half = ROPE // 2
    shared = np.concatenate([fl, z((D, NOPE - HEADS), f), k_pe, k_pe[:, half:], k_pe[:, :half]], 1)
    uq = swapped(i["w_uq"][0].reshape(384, HEADS, QK)).reshape(384, HEADS * P)
    ukv = i["w_ukv"][0].reshape(256, HEADS, NOPE + DV)
    k_up, v_up = ukv[..., :NOPE].reshape(256, -1), ukv[..., NOPE:].reshape(256, -1)
    attn = [units_by_tile(np.concatenate([shared, c_q, c_kv, fq, fk, fv], 1), 8),
            units_by_tile(k_up, 8), units_by_tile(v_up, 8), units_by_tile(uq, 8), z((1, 8, P, P), f)]
    gate_b, gate_c, u = np.split(i["w_in_conv"][0], 3, axis=1)

    def pairs(w):
        k, n = w.shape
        return w.reshape(k, 2, n // 2 // P, P).transpose(0, 2, 1, 3).reshape(k, n)
    a_u, a_v = np.split(i["a_w_in_2"][0], 2, axis=1)
    b_g, b_x = np.split(i["b_w_in_2"][0], 2, axis=1)
    wa, wx = i["b_w_a_2"][0], i["b_w_x_2"][0]
    gates = np.stack([np.concatenate([units_by_tile(wa[n], 2), units_by_tile(wx[n], 2)]).reshape(8, P, P)
                      for n in range(6)])
    eight = attn + [units_by_tile(np.concatenate(np.split(i["w_out_attn"][0], 2)[::-1]), 8),
                    units_by_tile(i["w_mlp_up"][0], 8), units_by_tile(i["w_mlp_down"][0], 8),
                    units_by_tile(np.concatenate([gate_c, u, gate_b], 1), 8), units_by_tile(i["w_out_conv"][0], 8),
                    units_by_tile(i["w_mlp_up"][1], 8), units_by_tile(i["w_mlp_down"][1], 8),
                    units_by_tile(a_v, 8), units_by_tile(a_u, 8), units_by_tile(i["a_w_out_2"][0], 8),
                    units_by_tile(pairs(i["f_w_up_2"][0]), 8),
                    units_by_tile(b_x, 8), gates, units_by_tile(b_g, 8), z((2, 8, P, P), f),
                    units_by_tile(pairs(i["f_w_up_2"][1]), 8)]
    six = [units_by_tile(i["f_w_down_2"][0], 6), units_by_tile(i["b_w_out_2"][0], 6),
           units_by_tile(i["f_w_down_2"][1], 6)]
    w8 = slabs_of(np.concatenate(eight))
    w6 = slabs_of(np.concatenate(six))

    def cols(a):
        a = a.reshape(-1, a.shape[-1])
        k, n = a.shape
        return a.reshape(k, n // P, P).transpose(2, 1, 0).reshape(P, -1)

    def pair_cols(a):
        a = a.reshape(-1, a.shape[-1])
        k, n = a.shape
        return cols(a.reshape(k, 2, n // 2 // P, P).transpose(0, 2, 1, 3).reshape(k, n))
    v = {
        "g_mix0": cols(i["g_mix"][0]), "g_mix1": cols(i["g_mix"][1]), "g_mlp0": cols(i["g_mlp"][0]),
        "g_mlp1": cols(i["g_mlp"][1]), "norm_mix0": cols(i["norm_mix_2"][0]), "norm_mix1": cols(i["norm_mix_2"][1]),
        "norm_ffn0": cols(i["norm_ffn_2"][0]), "norm_ffn1": cols(i["norm_ffn_2"][1]),
        "norm_final": cols(i["norm_final_2"]), "g_cq": cols(i["g_cq"]), "g_ckv": cols(i["g_ckv"]),
        "g_q_mla": swapped(i["g_q_mla"]).T, "g_k_mla": swapped(i["g_k_mla"]).T,
        "g_q_fox": pad_rows(i["g_q_fox"].T), "g_k_fox": pad_rows(i["g_k_fox"].T),
        "b_forget": pad_rows(i["b_forget"].T), "eps": np.full((P, 1), EPS, f), "conv_w": cols(i["conv_w"][0]),
        "v_gain": cols(i["a_v_gain_2"]), "b_conv_w": cols(i["b_conv_w_2"][0]), "b_conv_b": cols(i["b_conv_b_2"]),
        "b_b_a": cols(i["b_b_a_2"].reshape(-1)), "b_b_x": cols(i["b_b_x_2"].reshape(-1)),
        "lam": cols(i["b_lambda_2"]), "f_conv_w0": pair_cols(i["f_conv_w_2"][0]),
        "f_conv_b0": pair_cols(i["f_conv_b_2"][0]), "f_conv_w1": pair_cols(i["f_conv_w_2"][1]),
        "f_conv_b1": pair_cols(i["f_conv_b_2"][1]),
    }
    columns, _ = param_columns()
    assert all(v[n].shape == (P, k) for n, (_, k) in columns.items())
    params = np.concatenate([v[n] for n in columns], 1)

    pos = np.arange(T0, dtype=f)
    inv_freq = (10000.0 ** (-np.arange(0, ROPE, 2) / ROPE)).astype(f)
    ang = (pos[None, :] * inv_freq[:, None]).astype(f)
    cos, sin = np.cos(ang), np.sin(ang)
    consts = z((P, NCONST), f)
    consts[:, K_IDENT:K_IDENT + P] = np.eye(P)
    consts[:, K_MASK:K_MASK + P] = np.triu(np.full((P, P), NEG), 1)
    consts[:, K_ONES:K_ONES + P] = 1
    consts[64:96, K_ROPE:K_ROPE + T0] = np.concatenate([cos, cos])
    consts[96:128, K_ROPE:K_ROPE + T0] = np.concatenate([-sin, sin])
    consts[:, K_SEL:] = np.eye(HEADS).reshape(-1)
    rows = np.repeat(np.eye(HEADS, dtype=f)[:, :, None], P, 2)
    pad = z((2, FOX_K - 64, HEADS, T0), f)
    for hd in range(HEADS):
        pad[0, 32 + hd, hd] = -8
        pad[1, hd, hd] = 1

    x = np.concatenate([i["meta_tokens"], i["x"][0]], 0)
    return {
        "x_fm": x.T.reshape(KT, P, T0).transpose(1, 0, 2), "w8": w8, "w6": w6, "params_cols": params,
        "constants": consts, "head_rows": rows, "decay_rows": pad, "ws_src": i["a_w_s_2"][0].transpose(2, 0, 1).reshape(P, GROUPS * P),
        "bs_rows": np.repeat(i["a_b_s_2"], P, axis=0),
    }


def kernel(**inputs):
    import concourse.bacc as bacc
    from concourse.bass_utils import run_bass_kernel_spmd

    nc = bacc.Bacc("TRN2", target_bir_lowering=False, num_devices=1)
    arrays = {n: np.ascontiguousarray(a) for n, a in lay_out({k: np.asarray(v) for k, v in inputs.items()}).items()}
    args = [nc.dram_tensor(n, a.shape, mybir.dt.from_np(a.dtype), kind="ExternalInput").ap()
            for n, a in arrays.items()]
    args.append(nc.dram_tensor("out_fm", (P, KT, SEQ), F32, kind="ExternalOutput").ap())
    program(nc, *args)
    r = run_bass_kernel_spmd(nc, [arrays], core_ids=[0])
    got = r.results[0]["out_fm"]
    return got.transpose(1, 0, 2).reshape(D, SEQ).T.reshape(1, SEQ, D)
```
